# Optimizing a Trainium2 kernel written in Bass

```python
import math
import jax, jax.numpy as jnp
from jax import lax
import numpy as np

D_MODEL = 1024
BATCH = 1
SEQ = 128
DEPTH = 2
DEC_BATCH = 1
DEC_SEQ = 512
PAST_LEN = 128

GRID_W = 64
ATTN_WIDTH = 512
N_HEADS = 8
N_KV_HEADS = 2
HEAD_DIM = 64
GQA = N_HEADS // N_KV_HEADS
ROPE_THETA = 10000.0
ROT_PAIRS = HEAD_DIM // 4
Q_BLOCK = 128
SSM_WIDTH = 512
SSM_HEADS = 8
SSM_HEAD_DIM = 64
SSM_GROUPS = 2
SSM_STATE = 64
CONV_W = 5
CHUNK = 128
N_EXPERTS = 16
EC_FACTOR = 2
EXPERT_FF = 1024
EPS = 1e-6

MIX_WIDTH = ATTN_WIDTH + SSM_WIDTH
Q_DIM = N_HEADS * HEAD_DIM
KV_DIM = N_KV_HEADS * HEAD_DIM
BC_DIM = SSM_GROUPS * SSM_STATE
CONV_DIM = SSM_WIDTH + 2 * BC_DIM
IN_DIM = Q_DIM + 2 * KV_DIM + CONV_DIM + SSM_WIDTH + 2 * SSM_HEADS
SPLITS = (Q_DIM, Q_DIM + KV_DIM, Q_DIM + 2 * KV_DIM, Q_DIM + 2 * KV_DIM + CONV_DIM,
          Q_DIM + 2 * KV_DIM + CONV_DIM + SSM_WIDTH)

kernel_name = "hybrid_attn_ssd_ec_diffusion_step"

def rmsnorm(x, g):
    x32 = x.astype(jnp.float32)
    r = x32 * lax.rsqrt(jnp.mean(x32 * x32, axis=-1, keepdims=True) + EPS)
    return (r * g.astype(jnp.float32)).astype(x.dtype)

def axial_rope(length):
    t = jnp.arange(length)
    row = (t // GRID_W).astype(jnp.float32)
    col = (t % GRID_W).astype(jnp.float32)
    inv = ROPE_THETA ** (-jnp.arange(ROT_PAIRS, dtype=jnp.float32) / ROT_PAIRS)
    ang = jnp.concatenate([row[:, None] * inv, col[:, None] * inv], axis=-1)
    return jnp.cos(ang), jnp.sin(ang)

def apply_rope(x, cos, sin):
    half = HEAD_DIM // 2
    x32 = x.astype(jnp.float32)
    x1, x2 = x32[..., :half], x32[..., half:]
    c, s = cos[None, :, None, :], sin[None, :, None, :]
    return jnp.concatenate([x1 * c - x2 * s, x2 * c + x1 * s], axis=-1).astype(x.dtype)

def block_attention(q, keys, vals):
    b, L, _, d = q.shape
    nb = L // Q_BLOCK
    qb = q.astype(jnp.float32).reshape(b, nb, Q_BLOCK, N_KV_HEADS, GQA, d).transpose(1, 0, 2, 3, 4, 5)
    k32 = keys.astype(jnp.float32)
    v32 = vals.astype(jnp.float32)
    scale = HEAD_DIM ** -0.5

    def one_block(qblk):
        s = jnp.einsum('bqkgd,bskd->bkgqs', qblk, k32) * scale
        p = jax.nn.softmax(s, axis=-1)
        return jnp.einsum('bkgqs,bskd->bqkgd', p, v32)

    o = lax.map(one_block, qb)
    return o.transpose(1, 0, 2, 3, 4, 5).reshape(b, L, N_HEADS * d).astype(q.dtype)

def centred_dwconv(u, w, bias):
    pad = CONV_W // 2
    out = lax.conv_general_dilated(
        u, w[:, None, :].astype(u.dtype), window_strides=(1,), padding=[(pad, pad)],
        dimension_numbers=('NWC', 'WIO', 'NWC'), feature_group_count=u.shape[-1])
    return out + bias.astype(u.dtype)

def ssd_scan(x, dt, A, Bm, Cm, h0):
    b, L, H, P = x.shape
    nc = L // CHUNK
    rep = H // SSM_GROUPS
    xc = x.reshape(b, nc, CHUNK, H, P)
    Bc = jnp.repeat(Bm, rep, axis=2).reshape(b, nc, CHUNK, H, SSM_STATE)
    Cc = jnp.repeat(Cm, rep, axis=2).reshape(b, nc, CHUNK, H, SSM_STATE)
    dtc = dt.reshape(b, nc, CHUNK, H)
    acs = jnp.cumsum(dtc * A, axis=2)
    seg = acs[:, :, :, None, :] - acs[:, :, None, :, :]
    lower = jnp.tril(jnp.ones((CHUNK, CHUNK), dtype=bool))[None, None, :, :, None]
    decay = jnp.exp(jnp.where(lower, seg, -jnp.inf))
    scores = jnp.einsum('bcihn,bcjhn->bcijh', Cc, Bc) * decay * dtc[:, :, None, :, :]
    y_diag = jnp.einsum('bcijh,bcjhp->bcihp', scores, xc)
    w_end = jnp.exp(acs[:, :, -1:, :] - acs) * dtc
    states = jnp.einsum('bcjhn,bcjh,bcjhp->bchpn', Bc, w_end, xc)
    chunk_decay = jnp.exp(acs[:, :, -1, :])

    def step(h, inp):
        s, dcy = inp
        return h * dcy[:, :, None, None] + s, h

    h_final, h_prev = lax.scan(step, h0, (states.transpose(1, 0, 2, 3, 4), chunk_decay.transpose(1, 0, 2)))
    h_prev = h_prev.transpose(1, 0, 2, 3, 4)
    y_off = jnp.einsum('bcihn,bchpn,bcih->bcihp', Cc, h_prev, jnp.exp(acs))
    return (y_diag + y_off).reshape(b, L, H, P), h_final

def ssd_mixer(xbc, z, dt_raw, h0, A_log, dt_bias, d_skip, norm_g):
    b, L, _ = xbc.shape
    x32 = xbc.astype(jnp.float32)
    xs = x32[..., :SSM_WIDTH].reshape(b, L, SSM_HEADS, SSM_HEAD_DIM)
    Bm = x32[..., SSM_WIDTH:SSM_WIDTH + BC_DIM].reshape(b, L, SSM_GROUPS, SSM_STATE)
    Cm = x32[..., SSM_WIDTH + BC_DIM:].reshape(b, L, SSM_GROUPS, SSM_STATE)
    A = -jnp.exp(A_log.astype(jnp.float32))
    dt = jax.nn.softplus(dt_raw.astype(jnp.float32).reshape(b, L, 2, SSM_HEADS)
                         + dt_bias.astype(jnp.float32))
    h0 = h0.astype(jnp.float32)
    y_f, h_f = ssd_scan(xs, dt[:, :, 0], A[0], Bm, Cm, h0[:, 0])
    flip = lambda t: jnp.flip(t, axis=1)
    y_b, h_b = ssd_scan(flip(xs), flip(dt[:, :, 1]), A[1], flip(Bm), flip(Cm), h0[:, 1])
    y = y_f + flip(y_b) + xs * d_skip.astype(jnp.float32)[:, None]
    y = y.reshape(b, L, SSM_WIDTH) * jax.nn.silu(z.astype(jnp.float32))
    y = rmsnorm(y, norm_g).astype(xbc.dtype)
    return y, jnp.stack([h_f, h_b], axis=1)

def expert_choice_ffn(h, w_router, w_gate, w_up, w_down):
    b, L, D = h.shape
    n = b * L
    xs = h.reshape(n, D)
    aff = jax.nn.softmax(jnp.dot(xs, w_router).astype(jnp.float32), axis=-1)
    cap = EC_FACTOR * n // N_EXPERTS
    gates, idx = lax.top_k(aff.T, cap)
    xe = xs[idx]
    hid = jax.nn.silu(jnp.einsum('ecd,edf->ecf', xe, w_gate)) * jnp.einsum('ecd,edf->ecf', xe, w_up)
    ye = jnp.einsum('ecf,efd->ecd', hid, w_down) * gates[..., None].astype(h.dtype)
    out = jnp.zeros_like(xs).at[idx.reshape(-1)].add(ye.reshape(-1, D))
    return out.reshape(b, L, D)

def trunk_layer(x, cvec, rope, ctx, lp):
    b, L, _ = x.shape
    mod = jnp.dot(jax.nn.silu(cvec), lp['ada_w']) + lp['ada_b']
    sh1, sc1, g1, sh2, sc2, g2 = jnp.split(mod[:, None, :], 6, axis=-1)
    h = rmsnorm(x, lp['norm1']) * (1 + sc1) + sh1
    proj = jnp.dot(h, lp['w_in'])
    q, k, v, xbc, z, dt_raw = jnp.split(proj, SPLITS, axis=-1)
    q = rmsnorm(q.reshape(b, L, N_HEADS, HEAD_DIM), lp['q_norm'])
    k = rmsnorm(k.reshape(b, L, N_KV_HEADS, HEAD_DIM), lp['k_norm'])
    v = v.reshape(b, L, N_KV_HEADS, HEAD_DIM)
    if ctx is None:
        keys, vals = k, v
        h0 = jnp.zeros((b, 2, SSM_HEADS, SSM_HEAD_DIM, SSM_STATE), jnp.float32)
    else:
        cos, sin = rope
        q = apply_rope(q, cos, sin)
        k_lat = apply_rope(k, cos, sin)
        k_ctx, v_ctx, h0 = ctx
        keys = jnp.concatenate([k_ctx.astype(k.dtype), k_lat], axis=1)
        vals = jnp.concatenate([v_ctx.astype(v.dtype), v], axis=1)
    attn = block_attention(q, keys, vals)
    xbc = jax.nn.silu(centred_dwconv(xbc, lp['conv_w'], lp['conv_b']))
    ssm, h_fin = ssd_mixer(xbc, z, dt_raw, h0, lp['A_log'], lp['dt_bias'], lp['d_skip'], lp['ssm_norm'])
    x = x + g1 * jnp.dot(jnp.concatenate([attn, ssm], axis=-1), lp['w_out'])
    h2 = rmsnorm(x, lp['norm2']) * (1 + sc2) + sh2
    x = x + g2 * expert_choice_ffn(h2, lp['w_router'], lp['w_gate'], lp['w_up'], lp['w_down'])
    return x, k, v, h_fin

def setup_inputs(seed: int = 0) -> dict:
    key = jax.random.key(seed)
    ks = jax.random.split(key, 26)
    f32 = jnp.float32
    nrm = lambda k, shape, s: jax.random.normal(k, shape, f32) * s
    dt0 = jnp.exp(jax.random.uniform(ks[17], (DEPTH, 2, SSM_HEADS), f32, math.log(1e-3), math.log(1e-1)))
    return {
        "x_prompt": nrm(ks[0], (BATCH, SEQ, D_MODEL), 1.0),
        "x_sample": nrm(ks[1], (DEC_BATCH, DEC_SEQ, D_MODEL), 1.0),
        "cache_k": nrm(ks[2], (DEC_BATCH, DEPTH, PAST_LEN, N_KV_HEADS, HEAD_DIM), 1.0),
        "cache_v": nrm(ks[3], (DEC_BATCH, DEPTH, PAST_LEN, N_KV_HEADS, HEAD_DIM), 1.0),
        "state_ssm": nrm(ks[4], (DEC_BATCH, DEPTH, 2, SSM_HEADS, SSM_HEAD_DIM, SSM_STATE), 0.5),
        "c": nrm(ks[5], (DEC_BATCH, D_MODEL), 1.0),
        "c_ctx": nrm(ks[6], (D_MODEL,), 1.0),
        "norm1": 1.0 + nrm(ks[7], (DEPTH, D_MODEL), 0.02),
        "norm2": 1.0 + nrm(ks[8], (DEPTH, D_MODEL), 0.02),
        "ada_w": nrm(ks[9], (DEPTH, D_MODEL, 6 * D_MODEL), 0.5 * D_MODEL ** -0.5),
        "ada_b": nrm(ks[10], (DEPTH, 6 * D_MODEL), 0.02),
        "w_in": nrm(ks[11], (DEPTH, D_MODEL, IN_DIM), D_MODEL ** -0.5),
        "conv_w": nrm(ks[12], (DEPTH, CONV_W, CONV_DIM), CONV_W ** -0.5),
        "conv_b": nrm(ks[13], (DEPTH, CONV_DIM), 0.02),
        "q_norm": 1.0 + nrm(ks[14], (DEPTH, HEAD_DIM), 0.02),
        "k_norm": 1.0 + nrm(ks[15], (DEPTH, HEAD_DIM), 0.02),
        "A_log": jnp.log(jax.random.uniform(ks[16], (DEPTH, 2, SSM_HEADS), f32, 1.0, 16.0)),
        "dt_bias": dt0 + jnp.log(-jnp.expm1(-dt0)),
        "d_skip": 1.0 + nrm(ks[18], (DEPTH, SSM_HEADS), 0.1),
        "ssm_norm": 1.0 + nrm(ks[19], (DEPTH, SSM_WIDTH), 0.02),
        "w_out": nrm(ks[20], (DEPTH, MIX_WIDTH, D_MODEL), MIX_WIDTH ** -0.5),
        "w_router": nrm(ks[21], (DEPTH, D_MODEL, N_EXPERTS), D_MODEL ** -0.5),
        "w_gate": nrm(ks[22], (DEPTH, N_EXPERTS, D_MODEL, EXPERT_FF), D_MODEL ** -0.5),
        "w_up": nrm(ks[23], (DEPTH, N_EXPERTS, D_MODEL, EXPERT_FF), D_MODEL ** -0.5),
        "w_down": nrm(ks[24], (DEPTH, N_EXPERTS, EXPERT_FF, D_MODEL), EXPERT_FF ** -0.5),
    }

def reference(x_prompt, x_sample, cache_k, cache_v, state_ssm, c, c_ctx, norm1, norm2, ada_w, ada_b,
              w_in, conv_w, conv_b, q_norm, k_norm, A_log, dt_bias, d_skip, ssm_norm, w_out,
              w_router, w_gate, w_up, w_down):
    rope = axial_rope(x_sample.shape[1])
    cvec_ctx = c_ctx[None, :]
    y_prompt = x_prompt
    y_sample = x_sample
    ks_new, vs_new, hs_new = [], [], []
    for l in range(DEPTH):
        lp = {
            'norm1': norm1[l], 'norm2': norm2[l], 'ada_w': ada_w[l], 'ada_b': ada_b[l],
            'w_in': w_in[l], 'conv_w': conv_w[l], 'conv_b': conv_b[l], 'q_norm': q_norm[l],
            'k_norm': k_norm[l], 'A_log': A_log[l], 'dt_bias': dt_bias[l], 'd_skip': d_skip[l],
            'ssm_norm': ssm_norm[l], 'w_out': w_out[l], 'w_router': w_router[l],
            'w_gate': w_gate[l], 'w_up': w_up[l], 'w_down': w_down[l],
        }
        y_prompt, k_c, v_c, h_c = trunk_layer(y_prompt, cvec_ctx, None, None, lp)
        ks_new.append(k_c)
        vs_new.append(v_c)
        hs_new.append(h_c)
        ctx = (cache_k[:, l], cache_v[:, l], state_ssm[:, l])
        y_sample, _, _, _ = trunk_layer(y_sample, c, rope, ctx, lp)
    new_cache_k = jnp.stack(ks_new, axis=1)
    new_cache_v = jnp.stack(vs_new, axis=1)
    new_state_ssm = jnp.stack(hs_new, axis=1)
    return (y_prompt, y_sample, new_cache_k, new_cache_v, new_state_ssm)


_drawn_inputs = setup_inputs


def setup_inputs(seed=0):
    import zlib

    import numpy as np

    out = dict(_drawn_inputs(seed))
    spreads = {}
    factors = {'cache_k': 5.779,
     'cache_v': 5.293,
     'norm2': 5.68,
     'q_norm': 8.0,
     'k_norm': 2.805,
     'd_skip': 3.233,
     'ssm_norm': 7.247}
    for name, (base, spread) in spreads.items():
        noise = np.random.default_rng([zlib.crc32(name.encode()), seed]).standard_normal(out[name].shape)
        drawn = base * np.exp(spread * noise) if base else spread * noise
        out[name] = __import__('jax').numpy.asarray(drawn.astype(out[name].dtype))
    for name, factor in factors.items():
        out[name] = (out[name] * factor).astype(out[name].dtype)
    return out
```

```python
from contextlib import ExitStack

import numpy as np
import concourse.bass as bass
from concourse import mybir

F32 = mybir.dt.float32
I32 = mybir.dt.int32
U32 = mybir.dt.uint32
ALU = mybir.AluOpType
ACT = mybir.ActivationFunctionType
AX = mybir.AxisListType

P = 128
D = 1024
KD = D // P
LAYERS = 2
CTX, LAT = 128, 512
TOK = CTX + LAT
NT = TOK // P
HD = 64
HEADS, KVH = 8, 2
GQ = HEADS // KVH
XBC = 768
NC_ = XBC // P
CONV_W = 5
IN_DIM = 2064
C_Q, C_KV, C_XBC, C_Z, C_DT = 0, 512, 768, 1536, 2048
EXP = 16
CAP_L, CAP_C = 64, 16
SLOT = CAP_L + CAP_C
FF = 1024
EPS = 1e-6
GRID_W = 64
R_ADAB, R_N1, R_N2, R_SN, R_CB, R_CW, R_C, VROWS = 0, 48, 56, 64, 68, 74, 104, 120
B_QN, B_KN, B_AL, B_DTB, B_SK, BCOLS = 0, 64, 128, 144, 160, 168
SETS = ((0, 0, CTX), (1, CTX, LAT))
CW = 132
CL = CW + LAT
XL = CL + 4


def conv_cols(t):
    a = 0 if t == 0 else CW + (t - 1) * P
    return slice(a, a + P)


def build(nc, x_prompt, x_sample, cache_k, cache_v, state, vrows, bparams, rope, ada_w, w_in, w_out,
          w_router, w_gate, w_up, w_down, x_res, new_k, new_v, new_h):
    ctx = ExitStack()
    with ctx:
        def sb(name, shape, dt=F32):
            return ctx.enter_context(nc.sbuf_tensor(name, shape, dt))

        xn_dram = nc.dram_tensor("normed_rows", (TOK, D), F32, kind="Internal").ap()

        arena = sb("arena", [P, KD * IN_DIM + KD * D])
        RA = sb("RA", [P, NT * D])
        RB = sb("RB", [P, KD * TOK])
        RC = sb("RC", [P, NT * D])
        RD = sb("RD", [P, NT * 256])
        RE = sb("RE", [P, NC_ * XL])
        RF = sb("RF", [P, NC_ * CL])
        ident = sb("ident", [P, P])
        upto = sb("upto", [P, P])
        since = sb("since", [P, P])
        ones = sb("ones", [P, P])
        bars = sb("bars", [P, 2, P])
        ropes = sb("ropes", [P, NT, HD])
        vr = sb("vr", [P, P])
        vp = sb("vp", [P, VROWS])
        bp = sb("bp", [P, BCOLS])
        mod = sb("mod", [P, 48, 2])
        amp1 = sb("amp1", [P, KD, 2])
        amp2 = sb("amp2", [P, KD, 2])
        silc = sb("silc", [P, KD, 2])
        silt = sb("silt", [P, KD * 2])
        dtr = sb("dtr", [P, NT, 16])
        dt_ = sb("dt_", [P, NT, 16])
        adt = sb("adt", [P, NT, 16])
        dte = sb("dte", [P, NT, 16])
        dts = sb("dts", [P, NT, 16])
        negA = sb("negA", [P, 16])
        cs = sb("cs", [P, 4, NT, 8])
        ncs = sb("ncs", [P, 2, NT, 8])
        ecs = sb("ecs", [P, 2, NT, 8])
        wend = sb("wend", [P, 2, NT, 8])
        etot = sb("etot", [P, 2, NT, 8])
        cds = sb("cds", [P, 3, 2, GQ])
        ckv = sb("ckv", [P, 2, P])
        hst = sb("hst", [P, 2, 2, P])
        wr = sb("wr", [P, KD, EXP])
        ss = sb("ss", [P, 3, NT])
        rs = sb("rs", [P, 3, NT])
        hs = sb("hs", [P, NT, 10])
        mhalf = sb("mhalf", [P, NT * 10])
        nmax = sb("nmax", [P, 4])
        psum_ = sb("psum_", [P, 4])
        rinv = sb("rinv", [P, 4])
        aff = sb("aff", [P, NT, EXP])
        am = sb("am", [P, NT])
        top = sb("top", [P, 2, SLOT])
        topu = sb("topu", [EXP, SLOT], U32)
        col = sb("col", [SLOT, 2, EXP + 1])
        idx_g = sb("idx_g", [SLOT, 1], I32)
        idx_s = sb("idx_s", [SLOT, 1], I32)
        gcur = sb("gcur", [SLOT, 1])
        hold = sb("hold", [P, 1])
        pgate = sb("pgate", [P, 1])
        PS = ctx.enter_context(nc.psum_tensor("PS", [P, 8 * 512], F32))

        def bank(b, n=512):
            return PS[:, b * 512:b * 512 + n]

        x_t = RA[:, :].rearrange("p (t d) -> p t d", t=NT)
        cat = x_t
        hT = RB[:, :].rearrange("p (j s) -> p j s", j=KD)
        q_t = RC[:, 0:NT * 512].rearrange("p (t c) -> p t c", t=NT)
        z_t = RC[:, NT * 512:].rearrange("p (t c) -> p t c", t=NT)
        xr = RC[:, :].rearrange("p (t d) -> p t d", t=NT)
        kv_t = RD[:, :].rearrange("p (t c) -> p t c", t=NT)
        xin = RE[:, :].rearrange("p (c s) -> p c s", c=NC_)
        cv = RF[:, :].rearrange("p (c s) -> p c s", c=NC_)
        tokx = RE[:, 0:NT * 640].rearrange("p (t c) -> p t c", t=NT)
        qT = RE[:, 0:GQ * TOK].rearrange("p (m s) -> p m s", m=GQ)
        kT = RE[:, GQ * TOK:GQ * TOK + 768]
        g1b = RE[:, 0:2 * D].rearrange("p (s d) -> p s d", s=2)
        junk = RE[:, 2 * D:3 * D]
        optmp = RF[:, 0:D]
        hprev = RF[:, 0:2048].rearrange("p (s r c) -> p s r c", s=4, r=2)
        hctx = RF[:, 2048:2560].rearrange("p (r c) -> p r c", r=2)
        probs = RF[:, 0:1280].rearrange("p (i c) -> p i c", i=2)
        pT = RF[:, 1280:2560].rearrange("p (i c) -> p i c", i=2)
        EW = RB[:, 0:2048].rearrange("p (r c) -> p r c", r=2)
        xdt = RB[:, 2560:3584].rearrange("p (r c) -> p r c", r=2)
        xskip = RB[:, 3584:4608].rearrange("p (r c) -> p r c", r=2)
        ytmp = RB[:, 4608:5120]
        sqtmp = RF[:, 2048:2560]
        xw = [RB[:, 0:1024], RB[:, 1024:2048], RB[:, 2560:3584], RB[:, 3584:4608]]
        xg = RA[0:SLOT, 0:D]
        ys = RA[0:SLOT, D:2 * D]
        xeT = RA[:, 2048:2688]
        hid = RA[:, 2688:3328]
        sg = RA[:, 3328:3968]
        yT = RA[:, 3968:4608]
        wa = RE[0:EXP, 0:TOK]
        wb = RE[0:EXP, TOK:2 * TOK]

        class Signal:

            def __init__(self, name, per, unit=1):
                self.sem = ctx.enter_context(nc.semaphore(name))
                self.per, self.unit = per, unit

            def at(self, l, n):
                return l * (self.per * self.unit) + n * self.unit

        class Chain:

            def __init__(self, eng, name, per):
                self.eng, self.name, self.per, self.n = eng, name, per, 0
                self.sem = ctx.enter_context(nc.semaphore(name))

            def start(self, rnd):
                self.rnd, self.n = rnd, 0

            def link(self, ins):
                self.n += 1
                ins.then_inc(self.sem, 1)
                self.eng.wait_ge(self.sem, self.rnd * self.per + self.n)

            def end(self):
                assert self.n == self.per, f"{self.name}: {self.n} links, {self.per} stated"

        dve_consts = ctx.enter_context(nc.semaphore("dve_consts"))
        pool_consts = ctx.enter_context(nc.semaphore("pool_consts"))
        rope_in = ctx.enter_context(nc.semaphore("rope_in"))
        x_copied = ctx.enter_context(nc.semaphore("x_copied"))
        vec_in = Signal("vec_in", 2, 16)
        x_in = Signal("x_in", 1, 16)
        x2_in = Signal("x2_in", 1, 16)
        ckv_in = Signal("ckv_in", 2, 16)
        h0_in = Signal("h0_in", 8, 16)
        wr_in = Signal("wr_in", 1, 16)
        ada_in = [Signal(f"ada_in{i}", 2, 16) for i in range(4)]
        win_in = [Signal(f"win_in{i}", 1, 16) for i in range(2)]
        wout_in = Signal("wout_in", 1, 16)
        ew_in = [Signal(f"ew_in{i}", EXP, 16) for i in range(6)]
        ew_used = [Signal(f"ew_used{i}", EXP) for i in range(6)]
        vec_ps = Signal("vec_ps", 1)
        vp_rdy = Signal("vp_rdy", 1)
        silc_e = Signal("silc_e", 1)
        silc_rdy = Signal("silc_rdy", 1)
        ada_used = Signal("ada_used", 8)
        mod_rdy = Signal("mod_rdy", 1)
        ss_rdy = Signal("ss_rdy", 15)
        u_rdy = Signal("u_rdy", 15)
        rstd_rdy = Signal("rstd_rdy", 15)
        xn_rdy = Signal("xn_rdy", 15)
        tg_ps = Signal("tg_ps", 30)
        tg_dve = Signal("tg_dve", 15)
        tg_act = Signal("tg_act", 15)
        ip_ps = Signal("ip_ps", 27)
        ip_ev = Signal("ip_ev", 27)
        pads = Signal("pads", 1)
        tap0 = Signal("tap0", NC_)
        conv_rdy = Signal("conv_rdy", NC_)
        conv_e = Signal("conv_e", NC_)
        xs_rdy = Signal("xs_rdy", NC_)
        dt_abs = Signal("dt_abs", 1)
        dt_e = Signal("dt_e", 1)
        a_rdy = Signal("a_rdy", 1)
        cs_ps = Signal("cs_ps", 1)
        cs_rdy = Signal("cs_rdy", 1)
        cs_e = Signal("cs_e", 1)
        wend_rdy = Signal("wend_rdy", 1)
        h0_ps = Signal("h0_ps", 1)
        tok_ps = Signal("tok_ps", NT)
        tok_ev = Signal("tok_ev", NT)
        xw_rdy = Signal("xw_rdy", 4)
        S_ps = Signal("S_ps", 4)
        h_rdy = Signal("h_rdy", 4)
        hf_ps = Signal("hf_ps", 1)
        hf_ev = Signal("hf_ev", 1)
        G_ps = Signal("G_ps", 2 * NT)
        seg_ps = Signal("seg_ps", 2 * NT)
        m_rdy = Signal("m_rdy", 2 * NT)
        e_rdy = Signal("e_rdy", 2 * NT)
        w_rdy = Signal("w_rdy", 2 * NT)
        xdt_rdy = Signal("xdt_rdy", 2 * NT)
        skip_rdy = Signal("skip_rdy", NT)
        yd_ps = Signal("yd_ps", 2 * NT)
        y_ps = Signal("y_ps", NT - 1)
        y_done = Signal("y_done", NT)
        z_e = Signal("z_e", NT)
        z_rdy = Signal("z_rdy", NT)
        k_rdy = Signal("k_rdy", 1)
        k_out_rdy = Signal("k_out_rdy", 1)
        q_rdy = Signal("q_rdy", NT)
        qs_rdy = Signal("qs_rdy", 6)
        hsu_rdy = Signal("hsu_rdy", 1)
        hrs_rdy = Signal("hrs_rdy", 1)
        qkT_ps = Signal("qkT_ps", 6)
        qkT_act = Signal("qkT_act", 3)
        qkT_dve = Signal("qkT_dve", 3)
        UN = NT * HEADS
        s_ps = Signal("s_ps", UN)
        max_rdy = Signal("max_rdy", UN)
        p_rdy = Signal("p_rdy", UN)
        t_ps = Signal("t_ps", UN)
        pT_rdy = Signal("pT_rdy", UN)
        rinv_rdy = Signal("rinv_rdy", UN)
        o_ps = Signal("o_ps", UN)
        o_ev = Signal("o_ev", UN)
        g1_ps = Signal("g1_ps", 1)
        g1_rdy = Signal("g1_rdy", 1)
        op_ps = Signal("op_ps", NT)
        op_ev = Signal("op_ev", NT)
        x2_rdy = Signal("x2_rdy", NT)
        stored = Signal("stored", 2 * NT, 16)
        kv_out = Signal("kv_out", 2, 16)
        h_out = Signal("h_out", 8, 16)
        lg_ps = Signal("lg_ps", 1)
        lg_sub = Signal("lg_sub", 1)
        lg_e = Signal("lg_e", 1)
        aff_rdy = Signal("aff_rdy", 1)
        affT_ps = Signal("affT_ps", 1)
        top_rdy = Signal("top_rdy", 1)
        col_ps = Signal("col_ps", 1)
        col_rdy = Signal("col_rdy", 1)
        idx_rdy = Signal("idx_rdy", EXP + 1)
        idxs_rdy = Signal("idxs_rdy", EXP)
        held = Signal("held", 2 * EXP)
        gathered = Signal("gathered", EXP, 16)
        scattered = Signal("scattered", EXP, 16)
        xT_ps = Signal("xT_ps", EXP)
        xT_rdy = Signal("xT_rdy", EXP)
        eg_ps = ew_used[1]
        eu_ps = ew_used[3]
        ed_ps = ew_used[5]
        eg_e = Signal("eg_e", EXP)
        hid_rdy = Signal("hid_rdy", EXP)
        yT_rdy = Signal("yT_rdy", EXP)
        yt_ps = Signal("yt_ps", EXP)
        ys_rdy = Signal("ys_rdy", EXP)

        block = ctx.enter_context(nc.Block())

        def each_layer(eng):
            return eng.Fori(0, LAYERS)

        F_STEP = (0, 1, 2, 3)
        B_STEP = (0, 4, 3, 2)

        @block.sync
        def _(sp):
            sp.dma_start(x_res[0:CTX, :], x_prompt).then_inc(x_copied, 16)
            sp.dma_start(x_res[CTX:TOK, :], x_sample).then_inc(x_copied, 16)
            sp.dma_start(ropes[:, :, :], rope).then_inc(rope_in, 16)
            with each_layer(sp) as l:
                row = lambda a: a[bass.ds(l, 1)]
                sp.wait_ge(ew_used[0].sem, ew_used[0].at(l, 0))
                sp.dma_start(vr[0:VROWS, :], row(vrows).rearrange("a r c -> (a r) c")).then_inc(vec_in.sem, 16)
                sp.dma_start(bp[:, :], row(bparams).to_broadcast([P, BCOLS])).then_inc(vec_in.sem, 16)
                sp.dma_start(ckv[:, 0, :], row(cache_k).rearrange("a s c -> (a s) c")).then_inc(ckv_in.sem, 16)
                sp.dma_start(ckv[:, 1, :], row(cache_v).rearrange("a s c -> (a s) c")).then_inc(ckv_in.sem, 16)
                sp.dma_start(wr[:, :, :], row(w_router).rearrange("a (k p) e -> p (a k) e", p=P)).then_inc(wr_in.sem, 16)
                sp.wait_ge(h_out.sem, h_out.at(l, 0))
                for r in range(2):
                    for m in range(2):
                        for g in range(2):
                            h = g * GQ + 2 * m
                            src = row(state)[:, r, h:h + 2].rearrange("a h p n -> (a h p) n")
                            sp.dma_start(hst[:, r, m, g * HD:(g + 1) * HD], src).then_inc(h0_in.sem, 16)
                for c in range(8):
                    i = c % 4
                    if c < 4:
                        for j in ((1, 1, 3, 5)[c], (1, 3, 5, 5)[c]):
                            sp.wait_ge(ew_used[j].sem, ew_used[j].at(l, 0))
                    else:
                        sp.wait_ge(ada_used.sem, ada_used.at(l, c - 3))
                    sp.dma_start(arena[:, i * 6144:(i + 1) * 6144],
                                 row(ada_w)[:, c * P:(c + 1) * P, :].rearrange("a p n -> (a p) n")
                                 ).then_inc(ada_in[i].sem, 16)
                for hlf in range(2):
                    sp.wait_ge(ada_used.sem, ada_used.at(l, 6 + hlf))
                    k0 = hlf * 4
                    sp.dma_start(arena[:, k0 * IN_DIM:(k0 + 4) * IN_DIM].rearrange("p (k n) -> p k n", k=4),
                                 row(w_in)[:, k0 * P:(k0 + 4) * P, :].rearrange("a (k p) n -> p (a k) n", p=P)
                                 ).then_inc(win_in[hlf].sem, 16)
                sp.wait_ge(ada_used.sem, ada_used.at(l, 8))
                sp.dma_start(arena[:, KD * IN_DIM:].rearrange("p (k n) -> p k n", k=KD),
                             row(w_out).rearrange("a (k p) n -> p (a k) n", p=P)).then_inc(wout_in.sem, 16)
                def expert_half(E, j):
                    w = (w_gate, w_up, w_down)[j // 2]
                    k0 = (j % 2) * 4
                    sp.dma_start(arena[:, j * 4096:(j + 1) * 4096].rearrange("p (k n) -> p k n", k=4),
                                 w[bass.ds(E, 1), k0 * P:(k0 + 4) * P, :]
                                 .rearrange("a (k p) n -> p (a k) n", p=P)).then_inc(ew_in[j].sem, 16)

                for j in range(6):
                    if j == 0:
                        sp.wait_ge(ip_ps.sem, ip_ps.at(l, 27))
                    elif j == 4:
                        sp.wait_ge(op_ps.sem, op_ps.at(l, NT))
                    expert_half(l * EXP, j)
                with sp.Fori(1, EXP) as e:
                    for j in range(6):
                        sp.wait_ge(ew_used[j].sem, l * EXP + e)
                        expert_half(l * EXP + e, j)
            sp.wait_ge(x_copied, 32)
            sp.wait_ge(stored.sem, stored.at(LAYERS, 0))
            sp.wait_ge(kv_out.sem, kv_out.at(LAYERS, 0))
            sp.wait_ge(h_out.sem, h_out.at(LAYERS, 0))
            sp.wait_ge(scattered.sem, scattered.at(LAYERS, 0))

        @block.tensor
        def _(pe):
            mm = nc.tensor.matmul

            def transpose_groups(l, use, src, base):
                last = None
                for g in range(10):
                    if g >= 8:
                        s = (tg_dve, tg_act)[g % 2]
                        pe.wait_ge(s.sem, s.at(l, use * 5 + 1))
                    b = bank((base + g) % 8)
                    for i in range(4):
                        t, j = (1 + i, g) if g < 8 else (0, (g - 8) * 4 + i)
                        if g == 0:
                            pe.wait_ge(xn_rdy.sem, xn_rdy.at(l, use * NT + t + 1))
                        last = nc.tensor.transpose(b[:, i * P:(i + 1) * P], src[:, t, j * P:(j + 1) * P], ident[:, :])
                    last.then_inc(tg_ps.sem, 1)

            def transposed(l, use):
                pe.wait_ge(tg_dve.sem, tg_dve.at(l, use * 5 + 5))
                pe.wait_ge(tg_act.sem, tg_act.at(l, use * 5 + 5))

            def gate_or_up(E, j0, b0):
                last = None
                for hlf in range(2):
                    pe.wait_ge(ew_in[j0 + hlf].sem, E * 16 + 16)
                    for f in range(8):
                        o = (b0 + f // 4) * 512 + (f % 4) * SLOT
                        for k in range(4):
                            w = (j0 + hlf) * 4096 + k * FF + f * P
                            kk = hlf * 4 + k
                            src = hid if j0 == 4 else xeT
                            last = mm(PS[:, o:o + SLOT], arena[:, w:w + P], src[:, kk * SLOT:(kk + 1) * SLOT],
                                      start=(kk == 0 and f % 4 == 0), stop=(kk == 7), skip_group_check=True)
                    last.then_inc(ew_used[j0 + hlf].sem, 1)

            def tokens_in(E, l):
                pe.wait_ge(gathered.sem, E * 16 + 16)
                last = None
                for j in range(8):
                    o = (6 + j // 4) * 512 + (j % 4) * SLOT
                    last = nc.tensor.transpose(PS[:, o:o + SLOT], xg[:, j * P:(j + 1) * P], ident[0:SLOT, 0:SLOT])
                last.then_inc(xT_ps.sem, 1)

            def tokens_out(E):
                pe.wait_ge(yT_rdy.sem, E + 1)
                last = None
                for j in range(8):
                    o = 6 * 512 + j * P
                    last = nc.tensor.transpose(PS[0:SLOT, o:o + P], yT[:, j * SLOT:(j + 1) * SLOT], ident[:, :])
                last.then_inc(yt_ps.sem, 1)

            pe.wait_ge(dve_consts, 4)
            pe.wait_ge(pool_consts, 8)
            with each_layer(pe) as l:
                pe.wait_ge(vec_in.sem, vec_in.at(l, 2))
                nc.tensor.transpose(bank(0, VROWS), vr[0:VROWS, :], ident[0:VROWS, 0:VROWS]).then_inc(vec_ps.sem, 1)
                pe.wait_ge(silc_rdy.sem, silc_rdy.at(l, 1))
                last = None
                for c in range(8):
                    i = c % 4
                    pe.wait_ge(ada_in[i].sem, ada_in[i].at(l, c // 4 + 1))
                    for f in range(48):
                        last = mm(PS[:, 512 + 2 * f:514 + 2 * f], arena[:, i * 6144 + f * P:i * 6144 + (f + 1) * P],
                                  silc[:, c, :], start=(c == 0 and f == 0), stop=(c == 7), skip_group_check=True)
                    last.then_inc(ada_used.sem, 1)
                pe.wait_ge(mod_rdy.sem, mod_rdy.at(l, 1))
                transpose_groups(l, 0, x_t, 0)
                transposed(l, 0)

                pe.wait_ge(win_in[0].sem, win_in[0].at(l, 1))
                n = 0

                def project(parts):
                    nonlocal n
                    if n >= 8:
                        pe.wait_ge(ip_ev.sem, ip_ev.at(l, n - 7))
                    last = None
                    for o, wdt, lhs, rhs in parts:
                        for k in range(KD):
                            if n == 0 and k == 4:
                                pe.wait_ge(win_in[1].sem, win_in[1].at(l, 1))
                            last = mm(PS[:, (n % 8) * 512 + o:(n % 8) * 512 + o + wdt], lhs(k), rhs(k),
                                      start=(k == 0), stop=(k == KD - 1))
                    last.then_inc(ip_ps.sem, 1)
                    n += 1

                wcol = lambda k, a, w: arena[:, k * IN_DIM + a:k * IN_DIM + a + w]
                for c in range(NC_):
                    for _, s0, sn in (SETS[1], SETS[0]):
                        project([(0, sn, lambda k: wcol(k, C_XBC + c * P, P), lambda k: hT[:, k, s0:s0 + sn])])
                tokens = lambda t: (lambda k: hT[:, k, t * P:(t + 1) * P])
                for t in range(NT):
                    project([(0, 256, tokens(t), lambda k: wcol(k, C_KV, 256)),
                             (256, 16, tokens(t), lambda k: wcol(k, C_DT, 16))])
                for t in range(NT):
                    project([(0, 512, tokens(t), lambda k: wcol(k, C_Q, 512))])
                for t in range(NT):
                    project([(0, 512, tokens(t), lambda k: wcol(k, C_Z, 512))])

                pe.wait_ge(ip_ev.sem, ip_ev.at(l, 27))
                pe.wait_ge(a_rdy.sem, a_rdy.at(l, 1))
                mm(PS[:, 0:40], upto[:, :], adt[:, :, 0:8], start=True, stop=True)
                mm(PS[:, 40:80], since[:, :], adt[:, :, 8:16], start=True, stop=True)
                mm(PS[:, 80:120], ones[:, :], adt[:, :, 0:8], start=True, stop=True)
                mm(PS[:, 120:160], ones[:, :], adt[:, :, 8:16], start=True, stop=True).then_inc(cs_ps.sem, 1)
                pe.wait_ge(h0_in.sem, h0_in.at(l, 8))
                for r in range(2):
                    for m in range(2):
                        last = nc.tensor.transpose(PS[:, 512 + (2 * r + m) * P:512 + (2 * r + m + 1) * P],
                                                   hst[:, r, m, :], ident[:, :])
                last.then_inc(h0_ps.sem, 1)
                pe.wait_ge(xs_rdy.sem, xs_rdy.at(l, NC_))
                for t in range(NT):
                    b = 2 + 2 * (t % 3)
                    if t >= 3:
                        pe.wait_ge(tok_ev.sem, tok_ev.at(l, t - 2))
                    for c in range(5):
                        last = nc.tensor.transpose(PS[:, b * 512 + c * P:b * 512 + (c + 1) * P],
                                                   cv[:, c, conv_cols(t)], ident[:, :])
                    last.then_inc(tok_ps.sem, 1)
                pe.wait_ge(tok_ev.sem, tok_ev.at(l, NT))

                for s in range(4):
                    pe.wait_ge(xw_rdy.sem, xw_rdy.at(l, s + 1))
                    for r, t in ((0, F_STEP[s]), (1, B_STEP[s])):
                        for g in range(2):
                            o = (4 + s) * 512 + r * 256
                            last = mm(PS[g * HD:(g + 1) * HD, o:o + 256], tokx[:, t, 512 + g * HD:512 + (g + 1) * HD],
                                      xw[s][:, r * 512 + g * 256:r * 512 + (g + 1) * 256], start=True, stop=True)
                    last.then_inc(S_ps.sem, 1)

                def scores(t):
                    for g in range(2):
                        if t or g:
                            pe.wait_ge(G_ps.sem, G_ps.at(l, 2 * t + g))
                        mm(PS[:, g * P:(g + 1) * P], cv[g * HD:(g + 1) * HD, 4, conv_cols(t)],
                           cv[g * HD:(g + 1) * HD, 5, conv_cols(t)], start=True, stop=True).then_inc(G_ps.sem, 1)

                def cumulated(t):
                    for r in range(2):
                        if t:
                            pe.wait_ge(m_rdy.sem, m_rdy.at(l, 2 * (t - 1) + r + 1))
                        for h in range(8):
                            o = (2 + 2 * r) * 512 + h * P
                            last = nc.tensor.transpose(PS[:, o:o + P], cs[:, r, t, h:h + 1].to_broadcast([P, P]), ident[:, :])
                        last.then_inc(seg_ps.sem, 1)

                pe.wait_ge(h_rdy.sem, h_rdy.at(l, 4))
                cumulated(0)
                scores(0)
                for t in range(NT):
                    if t + 1 < NT:
                        cumulated(t + 1)
                    if t:
                        pe.wait_ge(y_done.sem, y_done.at(l, t))
                    for r in range(2):
                        pe.wait_ge(w_rdy.sem, w_rdy.at(l, 2 * t + r + 1))
                        pe.wait_ge(xdt_rdy.sem, xdt_rdy.at(l, 2 * t + r + 1))
                        for h in range(8):
                            last = mm(PS[:, 512 + h * HD:512 + (h + 1) * HD], EW[:, r, h * P:(h + 1) * P],
                                      xdt[:, r, h * HD:(h + 1) * HD], start=(r == 0 and h == 0), stop=(r == 1),
                                      skip_group_check=True)
                        last.then_inc(yd_ps.sem, 1)
                    if t + 1 < NT:
                        scores(t + 1)
                    if t:
                        for r, s in ((0, t - 1), (1, 4 - t)):
                            for g in range(2):
                                last = mm(PS[:, (6 + g) * 512 + r * 256:(6 + g) * 512 + (r + 1) * 256],
                                          cv[g * HD:(g + 1) * HD, 5, conv_cols(t)],
                                          hprev[g * HD:(g + 1) * HD, s, r, :], start=True, stop=True)
                        last.then_inc(y_ps.sem, 1)
                    else:
                        for r in range(2):
                            for m in range(2):
                                last = nc.tensor.transpose(PS[:, 3072 + (2 * r + m) * P:3072 + (2 * r + m + 1) * P],
                                                           hctx[:, r, m * P:(m + 1) * P], ident[:, :])
                        last.then_inc(hf_ps.sem, 1)
                        pe.wait_ge(hf_ev.sem, hf_ev.at(l, 1))

                pe.wait_ge(y_done.sem, y_done.at(l, NT))
                pe.wait_ge(k_rdy.sem, k_rdy.at(l, 1))
                pe.wait_ge(ckv_in.sem, ckv_in.at(l, 2))
                for i in range(6):
                    src = ckv[:, 0, :] if i == 1 else kv_t[:, (0, 0, 1, 2, 3, 4)[i], 0:P]
                    last = nc.tensor.transpose(PS[:, i * P:(i + 1) * P], src, ident[:, :])
                last.then_inc(qkT_ps.sem, 1)
                for t in range(NT):
                    pe.wait_ge(q_rdy.sem, q_rdy.at(l, t + 1))
                    for m in range(GQ):
                        o = (2 + t) * 512 + m * P
                        last = nc.tensor.transpose(PS[:, o:o + P], q_t[:, t, m * P:(m + 1) * P], ident[:, :])
                    last.then_inc(qkT_ps.sem, 1)
                pe.wait_ge(qkT_act.sem, qkT_act.at(l, 3))
                pe.wait_ge(qkT_dve.sem, qkT_dve.at(l, 3))

                def qk(u):
                    t, h = u // HEADS, u % HEADS
                    g, m = h // GQ, h % GQ
                    if u >= 2:
                        pe.wait_ge(p_rdy.sem, p_rdy.at(l, u - 1))
                    o = (u % 2) * 1024
                    for a, n_, k0 in (((0, 512, P), (512, 128, P + 512)) if t else ((0, P, 0),)):
                        last = mm(PS[:, o + a:o + a + n_], qT[g * HD:(g + 1) * HD, m, t * P:(t + 1) * P],
                                  kT[g * HD:(g + 1) * HD, k0:k0 + n_], start=True, stop=True)
                    last.then_inc(s_ps.sem, 1)

                qk(0)
                qk(1)
                for u in range(UN):
                    t, h = u // HEADS, u % HEADS
                    g = h // GQ
                    tiles = range(5 if t else 1)
                    pe.wait_ge(p_rdy.sem, p_rdy.at(l, u + 1))
                    if u:
                        pe.wait_ge(pT_rdy.sem, pT_rdy.at(l, u))
                    for i in tiles:
                        last = nc.tensor.transpose(PS[:, 2048 + i * P:2048 + (i + 1) * P],
                                                   probs[:, u % 2, i * P:(i + 1) * P], ident[:, :])
                    last.then_inc(t_ps.sem, 1)
                    if u + 2 < UN:
                        qk(u + 2)
                    pe.wait_ge(pT_rdy.sem, pT_rdy.at(l, u + 1))
                    if u >= 2:
                        pe.wait_ge(o_ev.sem, o_ev.at(l, u - 1))
                    for i in tiles:
                        v = (ckv[:, 1, :] if i == 0 else kv_t[:, i, P:2 * P]) if t else kv_t[:, 0, P:2 * P]
                        o = (6 + u % 2) * 512
                        last = mm(PS[:, o:o + HD], pT[:, u % 2, i * P:(i + 1) * P], v[:, g * HD:(g + 1) * HD],
                                  start=(i == 0), stop=(i == len(tiles) - 1))
                    last.then_inc(o_ps.sem, 1)

                pe.wait_ge(o_ev.sem, o_ev.at(l, UN))
                for s in range(2):
                    for j in range(KD):
                        o = (s * KD + j) * P
                        last = nc.tensor.transpose(PS[:, o:o + P], mod[:, 16 + j, s:s + 1].to_broadcast([P, P]), ident[:, :])
                last.then_inc(g1_ps.sem, 1)
                pe.wait_ge(g1_rdy.sem, g1_rdy.at(l, 1))
                transpose_groups(l, 1, cat, 4)
                transposed(l, 1)

                pe.wait_ge(wout_in.sem, wout_in.at(l, 1))
                for t in range(NT):
                    if t == 4:
                        pe.wait_ge(op_ev.sem, op_ev.at(l, 1))
                    for hlf in range(2):
                        for k in range(KD):
                            o = (t % 4) * 1024 + hlf * 512
                            w = KD * IN_DIM + k * D + hlf * 512
                            last = mm(PS[:, o:o + 512], hT[:, k, t * P:(t + 1) * P], arena[:, w:w + 512],
                                      start=(k == 0), stop=(k == KD - 1))
                    last.then_inc(op_ps.sem, 1)

                pe.wait_ge(op_ev.sem, op_ev.at(l, NT))
                transpose_groups(l, 2, x_t, 0)
                transposed(l, 2)
                pe.wait_ge(wr_in.sem, wr_in.at(l, 1))
                for t in range(NT):
                    for k in range(KD):
                        last = mm(PS[:, 1024 + t * EXP:1024 + (t + 1) * EXP], hT[:, k, t * P:(t + 1) * P], wr[:, k, :],
                                  start=(k == 0), stop=(k == KD - 1))
                last.then_inc(lg_ps.sem, 1)
                pe.wait_ge(aff_rdy.sem, aff_rdy.at(l, 1))
                for t in range(NT):
                    last = nc.tensor.transpose(PS[0:EXP, 2048 + t * P:2048 + (t + 1) * P], aff[:, t, :], ident[:, :])
                last.then_inc(affT_ps.sem, 1)
                pe.wait_ge(top_rdy.sem, top_rdy.at(l, 1))
                for i in range(2):
                    last = nc.tensor.transpose(PS[0:SLOT, 3072 + i * P:3072 + (i + 1) * P], top[:, i, :], ident[:, :])
                last.then_inc(col_ps.sem, 1)

                pe.wait_ge(col_rdy.sem, col_rdy.at(l, 1))
                tokens_in(l * EXP, l)
                pe.wait_ge(xT_rdy.sem, l * EXP + 1)
                gate_or_up(l * EXP, 0, 0)
                gate_or_up(l * EXP, 2, 2)
                with pe.Fori(1, EXP) as e:
                    E = l * EXP + e
                    tokens_in(E, l)
                    pe.wait_ge(hid_rdy.sem, E)
                    gate_or_up(E - 1, 4, 4)
                    pe.wait_ge(xT_rdy.sem, E + 1)
                    gate_or_up(E, 0, 0)
                    tokens_out(E - 1)
                    pe.wait_ge(ys_rdy.sem, E)
                    gate_or_up(E, 2, 2)
                E = l * EXP + EXP
                pe.wait_ge(hid_rdy.sem, E)
                gate_or_up(E - 1, 4, 4)
                tokens_out(E - 1)
                pe.wait_ge(ys_rdy.sem, E)

        @block.scalar
        def _(act):
            chain = Chain(act, "act_chain", 0)
            A = nc.scalar.activation

            def squares(l, use, t, src, out):
                if t:
                    act.wait_ge(ss_rdy.sem, ss_rdy.at(l, use * NT + t))
                A(out, src, ACT.Square, accum_out=ss[:, use, t:t + 1]).then_inc(ss_rdy.sem, 1)

            def move_groups(l, use, amp, shift):
                for g in range(1, 10, 2):
                    act.wait_ge(tg_ps.sem, tg_ps.at(l, use * 10 + g + 1))
                    b = bank(((0, 4, 0)[use] + g) % 8)
                    if g < 8:
                        put(hT[:, g, CTX:TOK], b, amp(g, 1), shift(g, 1)).then_inc(tg_act.sem, 1)
                    else:
                        for i in range(4):
                            last = put(hT[:, 4 + i, 0:CTX], b[:, i * P:(i + 1) * P], amp(4 + i, 0), shift(4 + i, 0))
                        last.then_inc(tg_act.sem, 1)

            def put(out, in_, a, s):
                if a is None:
                    return A(out, in_, ACT.Copy)
                if s is None:
                    return A(out, in_, ACT.Copy, scale=a)
                return A(out, in_, ACT.Identity, scale=a, bias=s)

            def gate_exp(E):
                act.wait_ge(eg_ps.sem, E + 1)
                act.wait_ge(hid_rdy.sem, E)
                A(sg.rearrange("p (b c) -> p b c", b=2), PS[:, 0:1024].rearrange("p (b c) -> p b c", b=2)[:, :, 0:320],
                  ACT.Exp, scale=-1.0).then_inc(eg_e.sem, 1)

            def rows_out(E):
                act.wait_ge(yt_ps.sem, E + 1)
                act.wait_ge(idxs_rdy.sem, E + 1)
                act.wait_ge(scattered.sem, E * 16)
                A(ys, PS[0:SLOT, 3072:4096], ACT.Copy, scale=gcur[:, 0:1]).then_inc(ys_rdy.sem, 1)

            act.wait_ge(x_copied, 32)
            with each_layer(act) as l:
                act.wait_ge(scattered.sem, scattered.at(l, 0))
                act.dma_start(x_t, x_res.rearrange("(t p) d -> p t d", p=P)).then_inc(x_in.sem, 16)
                act.wait_ge(vp_rdy.sem, vp_rdy.at(l, 1))
                A(silt[:, :], vp[:, R_C:R_C + 16], ACT.Exp, scale=-1.0).then_inc(silc_e.sem, 1)
                act.wait_ge(x_in.sem, x_in.at(l, 1))
                for t in range(NT):
                    squares(l, 0, t, x_t[:, t, :], optmp)
                act.wait_ge(mod_rdy.sem, mod_rdy.at(l, 1))
                move_groups(l, 0, lambda j, s: amp1[:, j, s:s + 1], lambda j, s: mod[:, j, s:s + 1])

                act.wait_ge(pads.sem, pads.at(l, 1))
                n = 0

                def evac(out, in_):
                    nonlocal n
                    act.wait_ge(ip_ps.sem, ip_ps.at(l, n + 1))
                    A(out, in_, ACT.Copy).then_inc(ip_ev.sem, 1)
                    n += 1

                def conv_exp(c):
                    act.wait_ge(conv_rdy.sem, conv_rdy.at(l, c + 1))
                    A(xin[:, c, 0:CL], cv[:, c, :], ACT.Exp, scale=-1.0).then_inc(conv_e.sem, 1)

                for c in range(NC_):
                    evac(xin[:, c, CW + 2:CW + 2 + LAT], bank(n % 8))
                    evac(xin[:, c, 2:2 + CTX], bank(n % 8, CTX))
                    act.wait_ge(ip_ev.sem, ip_ev.at(l, n))
                    A(cv[:, c, :], xin[:, c, 0:CL], ACT.Identity, scale=vp[:, R_CW + c:R_CW + c + 1],
                      bias=vp[:, R_CB + c:R_CB + c + 1]).then_inc(tap0.sem, 1)
                    if c:
                        conv_exp(c - 1)
                for t in range(NT):
                    b = bank(n % 8)
                    act.wait_ge(ip_ps.sem, ip_ps.at(l, n + 1))
                    A(kv_t[:, t, :], b[:, 0:256], ACT.Copy)
                    A(dtr[:, t, :], b[:, 256:272], ACT.Copy).then_inc(ip_ev.sem, 1)
                    n += 1
                conv_exp(NC_ - 1)
                A(negA[:, :], bp[:, B_AL:B_AL + 16], ACT.Exp)
                for t in range(NT):
                    b = bank(n % 8)
                    act.wait_ge(ip_ps.sem, ip_ps.at(l, n + 1))
                    A(q_t[:, t, :].rearrange("p (m g d) -> p g m d", m=GQ, g=KVH),
                      b.rearrange("p (g m d) -> p g m d", g=KVH, m=GQ), ACT.Copy).then_inc(ip_ev.sem, 1)
                    n += 1
                    if t == 0:
                        act.wait_ge(dt_abs.sem, dt_abs.at(l, 1))
                        A(dte[:, :, :], dts[:, :, :], ACT.Exp, scale=-1.0).then_inc(dt_e.sem, 1)
                for t in range(NT):
                    evac(z_t[:, t, :], bank(n % 8))
                for t in range(NT):
                    if t == 0:
                        act.wait_ge(ip_ev.sem, ip_ev.at(l, 27))
                        act.wait_ge(tg_ps.sem, tg_ps.at(l, 10))
                    A(RA[:, 2560 + t * 512:2560 + (t + 1) * 512], z_t[:, t, :], ACT.Exp, scale=-1.0).then_inc(z_e.sem, 1)

                act.wait_ge(cs_rdy.sem, cs_rdy.at(l, 1))
                A(ecs[:, :, :, :], cs[:, 0:2, :, :], ACT.Exp)
                A(etot[:, :, :, :], cs[:, 2:4, :, :], ACT.Exp)
                A(wend[:, :, :, :], wend[:, :, :, :], ACT.Exp).then_inc(cs_e.sem, 1)
                for t in range(NT):
                    act.wait_ge(tok_ps.sem, tok_ps.at(l, t + 1))
                    b = 2 + 2 * (t % 3)
                    A(tokx[:, t, :], PS[:, b * 512:b * 512 + 640], ACT.Copy).then_inc(tok_ev.sem, 1)
                for t in range(NT):
                    for r in range(2):
                        act.wait_ge(m_rdy.sem, m_rdy.at(l, 2 * t + r + 1))
                        A(EW[:, r, :], EW[:, r, :], ACT.Exp).then_inc(e_rdy.sem, 1)
                    if t == 0:
                        act.wait_ge(hf_ps.sem, hf_ps.at(l, 1))
                        act.wait_ge(h0_ps.sem, h0_ps.at(l, 1))
                        A(hst[:, :, :, :].rearrange("p r m c -> p (r m c)"), bank(6), ACT.Copy).then_inc(hf_ev.sem, 1)
                    if t:
                        act.wait_ge(y_done.sem, y_done.at(l, t))
                        squares(l, 1, t - 1, cat[:, t - 1, 512:1024], sqtmp)
                act.wait_ge(y_done.sem, y_done.at(l, NT))
                squares(l, 1, NT - 1, cat[:, NT - 1, 512:1024], sqtmp)
                act.wait_ge(hf_ev.sem, hf_ev.at(l, 1))
                for r in range(2):
                    for m in range(2):
                        for g in range(2):
                            h = g * GQ + 2 * m
                            dst = new_h[bass.ds(l, 1), r, h:h + 2].rearrange("a h p n -> (a h p) n")
                            act.dma_start(dst, hst[:, r, m, g * HD:(g + 1) * HD]).then_inc(h_out.sem, 16)
                act.wait_ge(k_rdy.sem, k_rdy.at(l, 1))
                act.dma_start(new_k[bass.ds(l, 1)].rearrange("a s c -> (a s) c"), kv_t[:, 0, 0:P]).then_inc(kv_out.sem, 16)
                act.dma_start(new_v[bass.ds(l, 1)].rearrange("a s c -> (a s) c"), kv_t[:, 0, P:2 * P]).then_inc(kv_out.sem, 16)
                act.wait_ge(qkT_ps.sem, qkT_ps.at(l, 1))
                A(kT, PS[:, 0:768], ACT.Copy).then_inc(qkT_act.sem, 1)
                for t in (3, 4):
                    act.wait_ge(qkT_ps.sem, qkT_ps.at(l, t + 2))
                    A(qT[:, :, t * P:(t + 1) * P], bank(2 + t).rearrange("p (m s) -> p m s", m=GQ), ACT.Copy).then_inc(qkT_act.sem, 1)
                act.wait_ge(qkT_ps.sem, qkT_ps.at(l, 6))
                act.wait_ge(y_done.sem, y_done.at(l, NT))
                act.dma_start(xr, x_res.rearrange("(t p) d -> p t d", p=P)).then_inc(x2_in.sem, 16)
                for u in range(UN + 2):
                    if u < UN:
                        n_ = 640 if u >= HEADS else P
                        act.wait_ge(max_rdy.sem, max_rdy.at(l, u + 1))
                        if u >= 2:
                            act.wait_ge(t_ps.sem, t_ps.at(l, u - 1))
                        if u >= 4:
                            act.wait_ge(rinv_rdy.sem, rinv_rdy.at(l, u - 3))
                        A(probs[:, u % 2, 0:n_], PS[:, (u % 2) * 1024:(u % 2) * 1024 + n_], ACT.Exp,
                          bias=nmax[:, u % 4:u % 4 + 1], accum_out=psum_[:, u % 4:u % 4 + 1]).then_inc(p_rdy.sem, 1)
                    if u >= 2:
                        v = u - 2
                        t, h = v // HEADS, v % HEADS
                        act.wait_ge(o_ps.sem, o_ps.at(l, v + 1))
                        act.wait_ge(rinv_rdy.sem, rinv_rdy.at(l, v + 1))
                        A(cat[:, t, h * HD:(h + 1) * HD], bank(6 + v % 2, HD), ACT.Copy,
                          scale=rinv[:, v % 4:v % 4 + 1]).then_inc(o_ev.sem, 1)
                act.wait_ge(g1_ps.sem, g1_ps.at(l, 1))
                A(g1b[:, 0, :], PS[:, 0:1024], ACT.Copy)
                A(g1b[:, 1, :], PS[:, 1024:2048], ACT.Copy).then_inc(g1_rdy.sem, 1)
                sn = lambda j, s: vp[:, R_SN + j - 4:R_SN + j - 3] if j >= 4 else None
                move_groups(l, 1, sn, lambda j, s: None)
                for t in range(NT):
                    act.wait_ge(x2_rdy.sem, x2_rdy.at(l, t + 1))
                    squares(l, 2, t, xr[:, t, :], junk)
                    act.dma_start(x_res[t * P:(t + 1) * P, :], xr[:, t, :]).then_inc(stored.sem, 16)
                    if t:
                        act.wait_ge(xn_rdy.sem, xn_rdy.at(l, 2 * NT + t))
                        act.dma_start(xn_dram[(t - 1) * P:t * P, :], x_t[:, t - 1, :]).then_inc(stored.sem, 16)
                act.wait_ge(xn_rdy.sem, xn_rdy.at(l, 3 * NT))
                act.dma_start(xn_dram[(NT - 1) * P:NT * P, :], x_t[:, NT - 1, :]).then_inc(stored.sem, 16)
                move_groups(l, 2, lambda j, s: amp2[:, j, s:s + 1], lambda j, s: mod[:, 24 + j, s:s + 1])
                act.wait_ge(lg_sub.sem, lg_sub.at(l, 1))
                A(aff[:, :, :], aff[:, :, :], ACT.Exp).then_inc(lg_e.sem, 1)
                gate_exp(l * EXP)
                with act.Fori(1, EXP) as e:
                    E = l * EXP + e
                    gate_exp(E)
                    rows_out(E - 1)
                rows_out(l * EXP + EXP - 1)

        @block.vector
        def _(dve):
            V = nc.vector
            chain = Chain(dve, "dve_chain", DVE_LINKS)
            first = Chain(dve, "dve_first", DVE_FIRST)
            loop = Chain(dve, "dve_loop", DVE_LOOP)
            tail = Chain(dve, "dve_tail", DVE_TAIL)
            link = chain.link

            def also(sig, ins, l, n):
                ins.then_inc(sig.sem, 1)
                dve.wait_ge(sig.sem, sig.at(l, n))

            def mean_eps(l, use, t, width):
                i = use * NT + t
                dve.wait_ge(ss_rdy.sem, ss_rdy.at(l, i + 1))
                V.tensor_scalar(rs[:, use, t:t + 1], ss[:, use, t:t + 1], 1.0 / width, EPS, ALU.mult, ALU.add).then_inc(u_rdy.sem, 1)

            def normed(l, use, t, out, src):
                i = use * NT + t
                dve.wait_ge(rstd_rdy.sem, rstd_rdy.at(l, i + 1))
                V.tensor_scalar(out, src, rs[:, use, t:t + 1], None, ALU.mult).then_inc(xn_rdy.sem, 1)

            def move_groups(l, use, amp, shift):
                for g in range(0, 10, 2):
                    dve.wait_ge(tg_ps.sem, tg_ps.at(l, use * 10 + g + 1))
                    b = bank(((0, 4, 0)[use] + g) % 8)
                    if g < 8:
                        put(hT[:, g, CTX:TOK], b, amp(g, 1), shift(g, 1)).then_inc(tg_dve.sem, 1)
                    else:
                        for i in range(4):
                            last = put(hT[:, i, 0:CTX], b[:, i * P:(i + 1) * P], amp(i, 0), shift(i, 0))
                        last.then_inc(tg_dve.sem, 1)

            def put(out, in_, a, s):
                if a is None:
                    return V.tensor_copy(out, in_)
                if s is None:
                    return V.tensor_scalar(out, in_, a, None, ALU.mult)
                return V.tensor_scalar(out, in_, a, s, ALU.mult, ALU.add)

            def column(ch, l, e, i, out, sig):
                ins = V.tensor_scalar(out, col[:, i, bass.ds(e, 1)] if not isinstance(e, int) else col[:, i, e:e + 1],
                                      1.0, None, ALU.mult)
                if sig:
                    ins.then_inc(sig.sem, 1)

            def tokens_in(ch, E):
                dve.wait_ge(xT_ps.sem, E + 1)
                src = PS[:, 3072:4096].rearrange("p (b c) -> p b c", b=2)[:, :, 0:320].rearrange("p b (j s) -> p b j s", s=SLOT)
                dst = xeT.rearrange("p (b j s) -> p b j s", b=2, s=SLOT)
                for st, a, n in ((1, 0, CAP_L), (0, CAP_L, CAP_C)):
                    amp = amp2[:, :, st:st + 1].rearrange("p (b j) s -> p b j s", b=2).broadcast_to([P, 2, 4, n])
                    V_ = V.tensor_tensor(dst[:, :, :, a:a + n], src[:, :, :, a:a + n], amp, ALU.mult)
                ch.link(V_)
                for st, a, n in ((1, 0, CAP_L), (0, CAP_L, CAP_C)):
                    sh = mod[:, 24:32, st:st + 1].rearrange("p (b j) s -> p b j s", b=2).broadcast_to([P, 2, 4, n])
                    V_ = V.tensor_tensor(dst[:, :, :, a:a + n], dst[:, :, :, a:a + n], sh, ALU.add)
                V_.then_inc(xT_rdy.sem, 1)

            def down_out(ch, E):
                dve.wait_ge(ed_ps.sem, E + 1)
                src = PS[:, 2048:3072].rearrange("p (b c) -> p b c", b=2)[:, :, 0:320].rearrange("p b (j s) -> p b j s", s=SLOT)
                dst = yT.rearrange("p (b j s) -> p b j s", b=2, s=SLOT)
                for st, a, n in ((1, 0, CAP_L), (0, CAP_L, CAP_C)):
                    g2 = mod[:, 40:48, st:st + 1].rearrange("p (b j) s -> p b j s", b=2).broadcast_to([P, 2, 4, n])
                    V_ = V.tensor_tensor(dst[:, :, :, a:a + n], src[:, :, :, a:a + n], g2, ALU.mult)
                V_.then_inc(yT_rdy.sem, 1)

            gu = lambda b: PS[:, b * 512:(b + 2) * 512].rearrange("p (b c) -> p b c", b=2)[:, :, 0:320]
            halves = lambda a: a.rearrange("p (b c) -> p b c", b=2)

            def silu_gate(ch, E):
                dve.wait_ge(eg_e.sem, E + 1)
                ch.link(V.tensor_scalar(sg, sg, 1.0, None, ALU.add))
                ch.link(V.reciprocal(sg, sg))
                ch.link(V.tensor_tensor(halves(sg), gu(0), halves(sg), ALU.mult))

            def times_up(ch, E):
                dve.wait_ge(eu_ps.sem, E + 1)
                V.tensor_tensor(halves(hid), gu(2), halves(sg), ALU.mult).then_inc(hid_rdy.sem, 1)

            V.memset(ones[:, :], 1.0).then_inc(dve_consts, 1)
            V.memset(mhalf[:, :], -0.5).then_inc(dve_consts, 1)
            V.memset(top[:, :, :], 0.0).then_inc(dve_consts, 1)
            V.memset(col[:, :, EXP:EXP + 1], 0.0).then_inc(dve_consts, 1)
            dve.wait_ge(dve_consts, 4)
            dve.wait_ge(rope_in, 16)
            dve.wait_ge(pool_consts, 8)
            with each_layer(dve) as l:
                chain.start(l)
                dve.wait_ge(vec_ps.sem, vec_ps.at(l, 1))
                also(vp_rdy, V.tensor_copy(vp[:, :], bank(0, VROWS)), l, 1)
                V.memset(xin[:, :, 0:2], 0.0)
                V.memset(xin[:, :, 2 + CTX:CW + 2], 0.0)
                V.memset(xin[:, :, CW + 2 + LAT:XL], 0.0).then_inc(pads.sem, 1)
                dve.wait_ge(silc_e.sem, silc_e.at(l, 1))
                link(V.tensor_scalar(silt[:, :], silt[:, :], 1.0, None, ALU.add))
                link(V.reciprocal(silt[:, :], silt[:, :]))
                V.tensor_tensor(silc[:, :, :].rearrange("p k s -> p s k"),
                                vp[:, R_C:R_C + 16].rearrange("p (s k) -> p s k", s=2),
                                silt[:, :].rearrange("p (s k) -> p s k", s=2), ALU.mult).then_inc(silc_rdy.sem, 1)
                for t in range(NT):
                    mean_eps(l, 0, t, D)
                for t in range(NT):
                    normed(l, 0, t, x_t[:, t, :], x_t[:, t, :])
                dve.wait_ge(ada_used.sem, ada_used.at(l, 8))
                link(V.tensor_tensor(mod[:, :, :], PS[:, 512:608].rearrange("p (f s) -> p f s", s=2),
                                     vp[:, 0:48].unsqueeze(2).broadcast_to([P, 48, 2]), ALU.add))
                V.scalar_tensor_tensor(amp1[:, :, :], mod[:, 8:16, :], 1.0,
                                       vp[:, R_N1:R_N1 + 8].unsqueeze(2).broadcast_to([P, 8, 2]), ALU.add, ALU.mult)
                also(mod_rdy, V.scalar_tensor_tensor(amp2[:, :, :], mod[:, 32:40, :], 1.0,
                                                     vp[:, R_N2:R_N2 + 8].unsqueeze(2).broadcast_to([P, 8, 2]), ALU.add, ALU.mult), l, 1)
                move_groups(l, 0, lambda j, s: amp1[:, j, s:s + 1], lambda j, s: mod[:, j, s:s + 1])

                def conv_silu(c):
                    dve.wait_ge(conv_e.sem, conv_e.at(l, c + 1))
                    link(V.tensor_scalar(xin[:, c, 0:CL], xin[:, c, 0:CL], 1.0, None, ALU.add))
                    link(V.reciprocal(xin[:, c, 0:CL], xin[:, c, 0:CL]))
                    V.tensor_tensor(cv[:, c, :], cv[:, c, :], xin[:, c, 0:CL], ALU.mult).then_inc(xs_rdy.sem, 1)

                for c in range(NC_):
                    dve.wait_ge(tap0.sem, tap0.at(l, c + 1))
                    for w in range(1, CONV_W):
                        r_ = R_CW + w * NC_ + c
                        ins = V.scalar_tensor_tensor(cv[:, c, :], xin[:, c, w:w + CL], vp[:, r_:r_ + 1], cv[:, c, :], ALU.mult, ALU.add)
                        if w < CONV_W - 1:
                            link(ins)
                    ins.then_inc(conv_rdy.sem, 1)
                    if c:
                        conv_silu(c - 1)
                conv_silu(NC_ - 1)

                dve.wait_ge(ip_ev.sem, ip_ev.at(l, 17))
                link(V.tensor_tensor(dtr[:, :, :], dtr[:, :, :], bp[:, B_DTB:B_DTB + 16].unsqueeze(1).broadcast_to([P, NT, 16]), ALU.add))
                link(V.tensor_scalar(dts[:, :, :], dtr[:, :, :], -1.0, None, ALU.mult))
                also(dt_abs, V.tensor_tensor(dts[:, :, :], dts[:, :, :], dtr[:, :, :], ALU.max), l, 1)
                dve.wait_ge(dt_e.sem, dt_e.at(l, 1))
                link(V.tensor_scalar(dts[:, :, :], dte[:, :, :], 2.0, None, ALU.add))
                link(V.reciprocal(dts[:, :, :], dts[:, :, :]))
                link(V.tensor_tensor(dts[:, :, :], dts[:, :, :], dte[:, :, :], ALU.mult))
                link(V.tensor_tensor(dte[:, :, :], dts[:, :, :], dts[:, :, :], ALU.mult))
                link(V.tensor_scalar(dt_[:, :, :], dte[:, :, :], 1.0 / 15, None, ALU.mult))
                for d in (13, 11, 9, 7, 5, 3):
                    link(V.scalar_tensor_tensor(dt_[:, :, :], dt_[:, :, :], 1.0 / d, dte[:, :, :], ALU.add, ALU.mult))
                link(V.scalar_tensor_tensor(dt_[:, :, :], dt_[:, :, :], 1.0, dts[:, :, :], ALU.add, ALU.mult))
                link(V.tensor_scalar(dtr[:, :, :], dtr[:, :, :], 0.0, None, ALU.max))
                link(V.scalar_tensor_tensor(dt_[:, :, :], dt_[:, :, :], 2.0, dtr[:, :, :], ALU.mult, ALU.add))
                V.scalar_tensor_tensor(adt[:, :, :], dt_[:, :, :], -1.0, negA[:, :].unsqueeze(1).broadcast_to([P, NT, 16]),
                                       ALU.mult, ALU.mult).then_inc(a_rdy.sem, 1)

                for t in range(NT):
                    dve.wait_ge(qs_rdy.sem, qs_rdy.at(l, t + 1))
                    V.tensor_reduce(hs[:, t, 0:8], RA[:, t * 512:(t + 1) * 512].rearrange("p (h d) -> p h d", d=HD), AX.X, ALU.add)
                dve.wait_ge(qs_rdy.sem, qs_rdy.at(l, 6))
                ksq = RB[:, 0:640].rearrange("p (t h d) -> p t h d", t=NT, h=KVH)
                link(V.tensor_reduce(hs[:, :, 8:10], ksq, AX.X, ALU.add))
                V.tensor_scalar(hs[:, :, :], hs[:, :, :], 1.0 / HD, EPS, ALU.mult, ALU.add).then_inc(hsu_rdy.sem, 1)
                dve.wait_ge(hrs_rdy.sem, hrs_rdy.at(l, 1))
                k4 = kv_t[:, :, 0:P].rearrange("p t (h d) -> p t h d", h=KVH)
                for h in range(KVH):
                    kh = k4[:, :, h, :]
                    link(V.tensor_tensor(kh, kh, hs[:, :, 8 + h:9 + h].broadcast_to([P, NT, HD]), ALU.mult))
                    link(V.tensor_tensor(kh, kh, bp[:, B_KN:B_KN + HD].unsqueeze(1).broadcast_to([P, NT, HD]), ALU.mult))
                    lo, hi = kh[:, :, 0:32], kh[:, :, 32:64]
                    co, si = ropes[:, :, 0:32], ropes[:, :, 32:64]
                    tm = [RB[:, 640 + i * 160:800 + i * 160].rearrange("p (t d) -> p t d", t=NT) for i in range(4)]
                    V.tensor_tensor(tm[0], lo, co, ALU.mult)
                    V.tensor_tensor(tm[1], hi, si, ALU.mult)
                    V.tensor_tensor(tm[2], hi, co, ALU.mult)
                    link(V.tensor_tensor(tm[3], lo, si, ALU.mult))
                    V.tensor_tensor(lo, tm[0], tm[1], ALU.subtract)
                    ins = V.tensor_tensor(hi, tm[2], tm[3], ALU.add)
                    if h == KVH - 1:
                        ins.then_inc(k_rdy.sem, 1)
                link(V.tensor_scalar(bp[:, B_QN:B_QN + HD], bp[:, B_QN:B_QN + HD], HD ** -0.5, None, ALU.mult))
                for t in range(NT):
                    qh = q_t[:, t, :].rearrange("p (h d) -> p h d", h=HEADS)
                    link(V.tensor_tensor(qh, qh, hs[:, t, 0:8].unsqueeze(2).broadcast_to([P, 8, HD]), ALU.mult))
                    link(V.tensor_tensor(qh, qh, bp[:, B_QN:B_QN + HD].unsqueeze(1).broadcast_to([P, 8, HD]), ALU.mult))
                    lo, hi = qh[:, :, 0:32], qh[:, :, 32:64]
                    co = ropes[:, t, 0:32].unsqueeze(1).broadcast_to([P, 8, 32])
                    si = ropes[:, t, 32:64].unsqueeze(1).broadcast_to([P, 8, 32])
                    tm = [RB[:, 1280 + i * 256:1536 + i * 256].rearrange("p (h d) -> p h d", h=8) for i in range(4)]
                    V.tensor_tensor(tm[0], lo, co, ALU.mult)
                    V.tensor_tensor(tm[1], hi, si, ALU.mult)
                    V.tensor_tensor(tm[2], hi, co, ALU.mult)
                    link(V.tensor_tensor(tm[3], lo, si, ALU.mult))
                    V.tensor_tensor(lo, tm[0], tm[1], ALU.subtract)
                    V.tensor_tensor(hi, tm[2], tm[3], ALU.add).then_inc(q_rdy.sem, 1)
                for t in range(NT):
                    dve.wait_ge(z_e.sem, z_e.at(l, t + 1))
                    e_ = RA[:, 2560 + t * 512:2560 + (t + 1) * 512]
                    link(V.tensor_scalar(e_, e_, 1.0, None, ALU.add))
                    link(V.reciprocal(e_, e_))
                    V.tensor_tensor(z_t[:, t, :], z_t[:, t, :], e_, ALU.mult).then_inc(z_rdy.sem, 1)
                dve.wait_ge(z_rdy.sem, z_rdy.at(l, NT))

                dve.wait_ge(cs_ps.sem, cs_ps.at(l, 1))
                link(V.tensor_copy(cs[:, :, :, :].rearrange("p a t h -> p (a t h)"), PS[:, 0:160]))
                V.tensor_scalar(ncs[:, :, :, :], cs[:, 0:2, :, :], -1.0, None, ALU.mult)
                V.tensor_tensor(wend[:, :, :, :], cs[:, 2:4, :, :], cs[:, 0:2, :, :], ALU.subtract).then_inc(cs_rdy.sem, 1)
                dve.wait_ge(cs_e.sem, cs_e.at(l, 1))
                for g in range(2):
                    rows = slice(g * HD, (g + 1) * HD)
                    for s in range(1, 4):
                        for r, t in ((0, F_STEP[s]), (1, B_STEP[s])):
                            V.tensor_copy(cds[rows, s - 1, r, :], etot[rows, r, t, g * GQ:(g + 1) * GQ])
                V.tensor_tensor(wend[:, :, :, :], wend[:, :, :, :], dt_[:, :, :].rearrange("p t (r h) -> p r t h", r=2),
                                ALU.mult).then_inc(wend_rdy.sem, 1)
                dve.wait_ge(h0_ps.sem, h0_ps.at(l, 1))
                dve.wait_ge(tok_ps.sem, tok_ps.at(l, NT))
                link(V.tensor_copy(hprev[:, 0, :, :].rearrange("p r c -> p (r c)"), bank(1)))
                for s in range(4):
                    dve.wait_ge(S_ps.sem, S_ps.at(l, s + 1))
                    if s == 0:
                        V.tensor_copy(hctx.rearrange("p r c -> p (r c)"), bank(4)).then_inc(h_rdy.sem, 1)
                        continue
                    dcy = cds[:, s - 1, :, :].rearrange("p r h -> p (r h)").unsqueeze(2).broadcast_to([P, 8, HD])
                    old = hprev[:, s - 1, :, :].rearrange("p r (h c) -> p (r h) c", c=HD)
                    new = hprev[:, s, :, :].rearrange("p r (h c) -> p (r h) c", c=HD)
                    link(V.tensor_tensor(new, old, dcy, ALU.mult))
                    also(h_rdy, V.tensor_tensor(new, new, bank(4 + s).rearrange("p (h c) -> p h c", c=HD), ALU.add), l, s + 1)

                def exponents(t):
                    for r in range(2):
                        dve.wait_ge(seg_ps.sem, seg_ps.at(l, 2 * t + r + 1))
                        if t:
                            dve.wait_ge(yd_ps.sem, yd_ps.at(l, 2 * (t - 1) + r + 1))
                        for h in range(8):
                            o = (2 + 2 * r) * 512 + h * P
                            ins = V.scalar_tensor_tensor(EW[:, r, h * P:(h + 1) * P], PS[:, o:o + P], ncs[:, r, t, h:h + 1],
                                                         bars[:, r, :], ALU.add, ALU.min)
                        ins.then_inc(m_rdy.sem, 1)

                def weights(t):
                    for r in range(2):
                        dve.wait_ge(e_rdy.sem, e_rdy.at(l, 2 * t + r + 1))
                        for g in range(2):
                            e_ = EW[:, r, g * 512:(g + 1) * 512].rearrange("p (h i) -> p h i", h=GQ)
                            o = g * P
                            ins = V.tensor_tensor(e_, e_, PS[:, o:o + P].unsqueeze(1).broadcast_to([P, GQ, P]), ALU.mult)
                        ins.then_inc(w_rdy.sem, 1)

                dve.wait_ge(S_ps.sem, S_ps.at(l, 4))
                exponents(0)
                for t in range(NT):
                    dve.wait_ge(G_ps.sem, G_ps.at(l, 2 * t + 2))
                    weights(t)
                    if t + 1 < NT:
                        exponents(t + 1)
                    y = cat[:, t, 512:1024]
                    byhead = lambda a: a.rearrange("p (h c) -> p h c", c=HD)
                    dve.wait_ge(yd_ps.sem, yd_ps.at(l, 2 * t + 2))
                    dve.wait_ge(skip_rdy.sem, skip_rdy.at(l, t + 1))
                    link(V.tensor_tensor(y, bank(1), xskip[:, t % 2, :], ALU.add))
                    if t:
                        dve.wait_ge(y_ps.sem, y_ps.at(l, t))
                        for r in range(2):
                            off = PS[:, 3072:4096].rearrange("p (g r c) -> p g r c", g=2, r=2)[:, :, r, :].rearrange("p g (h c) -> p g h c", c=HD)
                            link(V.tensor_tensor(ytmp.rearrange("p (g h c) -> p g h c", g=2, c=HD), off,
                                                 ecs[:, r, t, :].rearrange("p (g h) -> p g h", g=2).unsqueeze(3).broadcast_to([P, 2, GQ, HD]), ALU.mult))
                            link(V.tensor_tensor(y, y, ytmp, ALU.add))
                    V.tensor_tensor(y, y, z_t[:, t, :], ALU.mult).then_inc(y_done.sem, 1)
                for t in range(NT):
                    mean_eps(l, 1, t, 512)
                for t in range(3):
                    dve.wait_ge(qkT_ps.sem, qkT_ps.at(l, t + 2))
                    V.tensor_copy(qT[:, :, t * P:(t + 1) * P], bank(2 + t).rearrange("p (m s) -> p m s", m=GQ)).then_inc(qkT_dve.sem, 1)
                for u in range(UN + 1):
                    if u < UN:
                        n_ = 640 if u >= HEADS else P
                        dve.wait_ge(s_ps.sem, s_ps.at(l, u + 1))
                        if u >= 4:
                            dve.wait_ge(p_rdy.sem, p_rdy.at(l, u - 3))
                        V.tensor_reduce(nmax[:, u % 4:u % 4 + 1], PS[:, (u % 2) * 1024:(u % 2) * 1024 + n_], AX.X, ALU.max,
                                        negate=True).then_inc(max_rdy.sem, 1)
                    if u:
                        v = u - 1
                        n_ = 640 if v >= HEADS else P
                        dve.wait_ge(p_rdy.sem, p_rdy.at(l, v + 1))
                        if v >= 4:
                            dve.wait_ge(o_ev.sem, o_ev.at(l, v - 3))
                        V.reciprocal(rinv[:, v % 4:v % 4 + 1], psum_[:, v % 4:v % 4 + 1]).then_inc(rinv_rdy.sem, 1)
                        dve.wait_ge(t_ps.sem, t_ps.at(l, v + 1))
                        if v >= 2:
                            dve.wait_ge(o_ps.sem, o_ps.at(l, v - 1))
                        V.tensor_copy(pT[:, v % 2, 0:n_], PS[:, 2048:2048 + n_]).then_inc(pT_rdy.sem, 1)
                    if u in (8, 16, 24, 32, 36):
                        t = (8, 16, 24, 32, 36).index(u)
                        normed(l, 1, t, cat[:, t, 512:1024], cat[:, t, 512:1024])
                sn = lambda j, s: vp[:, R_SN + j - 4:R_SN + j - 3] if j >= 4 else None
                move_groups(l, 1, sn, lambda j, s: None)
                dve.wait_ge(x2_in.sem, x2_in.at(l, 1))
                dve.wait_ge(g1_rdy.sem, g1_rdy.at(l, 1))
                for t in range(NT):
                    dve.wait_ge(op_ps.sem, op_ps.at(l, t + 1))
                    also(op_ev, V.tensor_tensor(optmp, PS[:, (t % 4) * 1024:(t % 4) * 1024 + 1024], g1b[:, 1 if t else 0, :], ALU.mult), l, t + 1)
                    also(x2_rdy, V.tensor_tensor(xr[:, t, :], xr[:, t, :], optmp, ALU.add), l, t + 1)
                    if t:
                        mean_eps(l, 2, t - 1, D)
                        normed(l, 2, t - 1, x_t[:, t - 1, :], xr[:, t - 1, :])
                mean_eps(l, 2, NT - 1, D)
                normed(l, 2, NT - 1, x_t[:, NT - 1, :], xr[:, NT - 1, :])
                move_groups(l, 2, lambda j, s: amp2[:, j, s:s + 1], lambda j, s: mod[:, 24 + j, s:s + 1])

                dve.wait_ge(lg_ps.sem, lg_ps.at(l, 1))
                lg = PS[:, 1024:1024 + NT * EXP].rearrange("p (t e) -> p t e", t=NT)
                wide = am[:, :].unsqueeze(2).broadcast_to([P, NT, EXP])
                link(V.tensor_reduce(am[:, :], lg, AX.X, ALU.max))
                V.tensor_tensor(aff[:, :, :], lg, wide, ALU.subtract).then_inc(lg_sub.sem, 1)
                dve.wait_ge(lg_e.sem, lg_e.at(l, 1))
                link(V.tensor_reduce(am[:, :], aff[:, :, :], AX.X, ALU.add))
                link(V.reciprocal(am[:, :], am[:, :]))
                V.tensor_tensor(aff[:, :, :], aff[:, :, :], wide, ALU.mult).then_inc(aff_rdy.sem, 1)
                dve.wait_ge(affT_ps.sem, affT_ps.at(l, 1))
                link(V.tensor_copy(wa, PS[0:EXP, 2048:2048 + TOK]))
                V.memset(hold[:, :], 0.0)
                for st, a, n, rounds, s0 in ((1, CTX, LAT, CAP_L // 8, 0), (0, 0, CTX, CAP_C // 8, CAP_L)):
                    cur, nxt = wa, wb
                    for i in range(rounds):
                        o = s0 + 8 * i
                        link(V.max(top[0:EXP, 0, o:o + 8], cur[:, a:a + n]))
                        V.memset(hold[:, :], 0.0)
                        if i + 1 < rounds:
                            ins = V.match_replace(nxt[:, a:a + n], top[0:EXP, 0, o:o + 8], cur[:, a:a + n], -1.0)
                            V.max_index(topu[:, o:o + 8], top[0:EXP, 0, o:o + 8], cur[:, a:a + n])
                            link(ins)
                            V.memset(hold[:, :], 0.0)
                        else:
                            link(V.max_index(topu[:, o:o + 8], top[0:EXP, 0, o:o + 8], cur[:, a:a + n]))
                            V.memset(hold[:, :], 0.0)
                        cur, nxt = nxt, cur
                V.tensor_scalar(top[0:EXP, 1, 0:CAP_L], topu[:, 0:CAP_L], float(CTX), None, ALU.add)
                V.tensor_scalar(top[0:EXP, 1, CAP_L:SLOT], topu[:, CAP_L:SLOT], 0.0, None, ALU.add).then_inc(top_rdy.sem, 1)
                dve.wait_ge(col_ps.sem, col_ps.at(l, 1))
                also(col_rdy, V.tensor_copy(col[:, :, 0:EXP], PS[0:SLOT, 3072:3328].rearrange("p (i e) -> p i e", i=2)[:, :, 0:EXP]), l, 1)
                chain.end()

                E = l * EXP
                first.start(l)
                column(first, l, 0, 1, idx_g[:, :], idx_rdy)
                tokens_in(first, E)
                silu_gate(first, E)
                column(first, l, 1, 1, idx_g[:, :], idx_rdy)
                times_up(first, E)
                first.end()
                with dve.Fori(1, EXP) as e:
                    E = l * EXP + e
                    loop.start(l * (EXP - 1) + e - 1)
                    tokens_in(loop, E)
                    dve.wait_ge(scattered.sem, (E - 1) * 16)
                    column(loop, l, e - 1, 1, idx_s[:, :], None)
                    column(loop, l, e - 1, 0, gcur[:, :], idxs_rdy)
                    down_out(loop, E - 1)
                    silu_gate(loop, E)
                    column(loop, l, e + 1, 1, idx_g[:, :], idx_rdy)
                    times_up(loop, E)
                    loop.end()
                E = l * EXP + EXP
                tail.start(l)
                dve.wait_ge(scattered.sem, (E - 1) * 16)
                column(tail, l, EXP - 1, 1, idx_s[:, :], None)
                column(tail, l, EXP - 1, 0, gcur[:, :], idxs_rdy)
                down_out(tail, E - 1)
                tail.end()

        @block.gpsimd
        def _(pool):
            G = nc.gpsimd
            TT = G.tensor_tensor
            chain = Chain(pool, "pool_chain", POOL_LINKS)

            def hold_here(before):
                pool.wait_ge(held.sem, before)
                TT(pgate[:, :], pgate[:, :], pgate[:, :], ALU.add).then_inc(held.sem, 1)

            G.memset(pgate[:, :], 0.0).then_inc(pool_consts, 1)
            G.memset(ident[:, :], 0.0).then_inc(pool_consts, 1)
            pool.wait_ge(pool_consts, 2)
            pool.wait_ge(dve_consts, 4)
            G.affine_select(out=ident[:, :], in_=ident[:, :], compare_op=ALU.not_equal, fill=1.0, base=0,
                            pattern=[[-1, P]], channel_multiplier=1).then_inc(pool_consts, 1)
            G.affine_select(out=upto[:, :], in_=ones[:, :], compare_op=ALU.is_ge, fill=0.0, base=0,
                            pattern=[[1, P]], channel_multiplier=-1).then_inc(pool_consts, 1)
            G.affine_select(out=since[:, :], in_=ones[:, :], compare_op=ALU.is_ge, fill=0.0, base=0,
                            pattern=[[-1, P]], channel_multiplier=1).then_inc(pool_consts, 1)
            G.memset(bars[:, :, :], 0.0).then_inc(pool_consts, 1)
            pool.wait_ge(pool_consts, 6)
            for r in range(2):
                G.affine_select(out=bars[:, r, :], in_=bars[:, r, :], compare_op=ALU.is_ge, fill=-1e30, base=0,
                                pattern=[[1 - 2 * r, P]], channel_multiplier=2 * r - 1).then_inc(pool_consts, 1)
            pool.wait_ge(pool_consts, 8)

            def root(l, use, t):
                i = use * NT + t
                pool.wait_ge(u_rdy.sem, u_rdy.at(l, i + 1))
                TT(rs[:, use, t:t + 1], rs[:, use, t:t + 1], mhalf[:, 0:1], ALU.pow).then_inc(rstd_rdy.sem, 1)

            def gather():
                G.indirect_dma_start(out=xg, out_offset=None, in_=xn_dram[:, :],
                                     in_offset=bass.IndirectOffsetOnAxis(ap=idx_g[:, 0:1], axis=0),
                                     ).then_inc(gathered.sem, 16)

            def scatter(E, final=False):
                pool.wait_ge(ys_rdy.sem, E + 1)
                pool.wait_ge(scattered.sem, E * 16)
                hold_here(2 * E + 1 + (0 if final else 1))
                G.indirect_dma_start(out=x_res[:, :], out_offset=bass.IndirectOffsetOnAxis(ap=idx_s[:, 0:1], axis=0),
                                     in_=ys, in_offset=None, compute_op=ALU.add).then_inc(scattered.sem, 16)

            with each_layer(pool) as l:
                chain.start(l)
                for t in range(NT):
                    root(l, 0, t)
                pool.wait_ge(ip_ps.sem, ip_ps.at(l, 27))
                for t in range(NT):
                    pool.wait_ge(ip_ev.sem, ip_ev.at(l, 18 + t))
                    TT(RA[:, t * 512:(t + 1) * 512], q_t[:, t, :], q_t[:, t, :], ALU.mult).then_inc(qs_rdy.sem, 1)
                TT(RB[:, 0:640].rearrange("p (t c) -> p t c", t=NT), kv_t[:, :, 0:P], kv_t[:, :, 0:P], ALU.mult).then_inc(qs_rdy.sem, 1)
                pool.wait_ge(hsu_rdy.sem, hsu_rdy.at(l, 1))
                TT(hs[:, :, :].rearrange("p t h -> p (t h)"), hs[:, :, :].rearrange("p t h -> p (t h)"), mhalf[:, :], ALU.pow).then_inc(hrs_rdy.sem, 1)
                byhead = lambda a: a.rearrange("p (h c) -> p h c", c=HD)
                pool.wait_ge(wend_rdy.sem, wend_rdy.at(l, 1))
                pool.wait_ge(tok_ev.sem, tok_ev.at(l, NT))
                pool.wait_ge(q_rdy.sem, q_rdy.at(l, NT))
                for s in range(4):
                    for r, t in ((0, F_STEP[s]), (1, B_STEP[s])):
                        last = TT(byhead(xw[s][:, r * 512:(r + 1) * 512]), byhead(tokx[:, t, 0:512]),
                                  wend[:, r, t, :].unsqueeze(2).broadcast_to([P, 8, HD]), ALU.mult)
                    last.then_inc(xw_rdy.sem, 1)
                pool.wait_ge(S_ps.sem, S_ps.at(l, 4))
                for t in range(NT):
                    for r in range(2):
                        if t:
                            pool.wait_ge(yd_ps.sem, yd_ps.at(l, 2 * (t - 1) + r + 1))
                        TT(byhead(xdt[:, r, :]), byhead(tokx[:, t, 0:512]),
                           dt_[:, t, r * 8:(r + 1) * 8].unsqueeze(2).broadcast_to([P, 8, HD]), ALU.mult).then_inc(xdt_rdy.sem, 1)
                    if t >= 2:
                        pool.wait_ge(y_done.sem, y_done.at(l, t - 1))
                    TT(byhead(xskip[:, t % 2, :]), byhead(tokx[:, t, 0:512]),
                       bp[:, B_SK:B_SK + 8].unsqueeze(2).broadcast_to([P, 8, HD]), ALU.mult).then_inc(skip_rdy.sem, 1)
                for t in range(NT):
                    root(l, 1, t)
                for t in range(NT):
                    root(l, 2, t)
                chain.end()
                pool.wait_ge(stored.sem, stored.at(l, 2 * NT))
                pool.wait_ge(tg_ps.sem, tg_ps.at(l, 30))
                pool.wait_ge(idx_rdy.sem, idx_rdy.at(l, 1))
                hold_here(held.at(l, 0))
                gather()
                with pool.Fori(1, EXP) as e:
                    E = l * EXP + e
                    pool.wait_ge(xT_ps.sem, E)
                    pool.wait_ge(idx_rdy.sem, idx_rdy.at(l, 1) + e)
                    hold_here(2 * E - 1)
                    gather()
                    scatter(E - 1)
                scatter(l * EXP + EXP - 1, final=True)


DVE_LINKS, DVE_FIRST, DVE_LOOP, DVE_TAIL, POOL_LINKS = 132, 4, 4, 0, 0


def rope_table():
    t = np.arange(LAT)
    inv = (10000.0 ** (-np.arange(16, dtype=np.float32) / np.float32(16))).astype(np.float32)
    ang = np.concatenate([(t // GRID_W).astype(np.float32)[:, None] * inv,
                          (t % GRID_W).astype(np.float32)[:, None] * inv], axis=1)
    tab = np.zeros((TOK, 64), np.float32)
    tab[:, 0:32] = 1.0
    tab[CTX:, 0:32] = np.cos(ang)
    tab[CTX:, 32:64] = np.sin(ang)
    return np.ascontiguousarray(tab.reshape(NT, P, 64).transpose(1, 0, 2))


def kernel(**inputs):
    import concourse.bacc as bacc
    from concourse.bass_utils import run_bass_kernel_spmd

    a = {k: np.asarray(v) for k, v in inputs.items()}
    L = LAYERS
    both = lambda v: np.broadcast_to(v.reshape(1, 8, P), (L, 8, P))
    arrays = {
        "x_prompt": a["x_prompt"].reshape(CTX, D),
        "x_sample": a["x_sample"].reshape(LAT, D),
        "cache_k": a["cache_k"].reshape(L, P, P),
        "cache_v": a["cache_v"].reshape(L, P, P),
        "state": a["state_ssm"].reshape(L, 2, HEADS, HD, HD),
        "vrows": np.concatenate([
            a["ada_b"].reshape(L, 48, P), a["norm1"].reshape(L, 8, P), a["norm2"].reshape(L, 8, P),
            a["ssm_norm"].reshape(L, 4, P), a["conv_b"].reshape(L, NC_, P),
            a["conv_w"].reshape(L, CONV_W * NC_, P), both(a["c_ctx"]), both(a["c"])], axis=1),
        "bparams": np.concatenate([
            a["q_norm"], a["k_norm"], a["A_log"].reshape(L, 16), a["dt_bias"].reshape(L, 16), a["d_skip"]], axis=1),
        "rope": rope_table(),
        "ada_w": a["ada_w"], "w_in": a["w_in"], "w_out": a["w_out"], "w_router": a["w_router"],
        "w_gate": a["w_gate"].reshape(L * EXP, D, FF), "w_up": a["w_up"].reshape(L * EXP, D, FF),
        "w_down": a["w_down"].reshape(L * EXP, FF, D),
    }
    arrays = {k: np.ascontiguousarray(v) for k, v in arrays.items()}
    outs = {"x_res": (TOK, D), "new_k": (L, P, P), "new_v": (L, P, P), "new_h": (L, 2, HEADS, HD, HD)}
    nc = bacc.Bacc("TRN2", target_bir_lowering=False, num_devices=1)
    args = [nc.dram_tensor(k, v.shape, F32, kind="ExternalInput").ap() for k, v in arrays.items()]
    args += [nc.dram_tensor(k, s, F32, kind="ExternalOutput").ap() for k, s in outs.items()]
    build(nc, *args)
    r = run_bass_kernel_spmd(nc, [arrays], core_ids=[0]).results[0]
    x = np.asarray(r["x_res"])
    return (x[0:CTX].reshape(1, CTX, D), x[CTX:TOK].reshape(1, LAT, D),
            np.asarray(r["new_k"]).reshape(1, L, CTX, KVH, HD), np.asarray(r["new_v"]).reshape(1, L, CTX, KVH, HD),
            np.asarray(r["new_h"]).reshape(1, L, 2, HEADS, HD, HD))
```

```python
from contextlib import ExitStack

import numpy as np
import concourse.bass as bass
from concourse import mybir

F32 = mybir.dt.float32
F32R = mybir.dt.float32r
I32 = mybir.dt.int32
U32 = mybir.dt.uint32
ALU = mybir.AluOpType
ACT = mybir.ActivationFunctionType
AX = mybir.AxisListType

P = 128
D = 1024
KD = D // P
LAYERS = 2
CTX, LAT = 128, 512
TOK = CTX + LAT
NT = TOK // P
HD = 64
HEADS, KVH = 8, 2
GQ = HEADS // KVH
XBC = 768
NC_ = XBC // P
CONV_W = 5
IN_DIM = 2064
C_Q, C_KV, C_XBC, C_Z, C_DT = 0, 512, 768, 1536, 2048
EXP = 16
CAP_L, CAP_C = 64, 16
SLOT = CAP_L + CAP_C
FF = 1024
EPS = 1e-6
GRID_W = 64
R_ADAB, R_N1, R_N2, R_SN, R_CB, R_CW, R_C, VROWS = 0, 48, 56, 64, 68, 74, 104, 120
B_QN, B_KN, B_AL, B_DTB, B_SK, BCOLS = 0, 64, 128, 144, 160, 168
SETS = ((0, 0, CTX), (1, CTX, LAT))
CW = 132
CL = CW + LAT
XL = CL + 4


def conv_cols(t):
    a = 0 if t == 0 else CW + (t - 1) * P
    return slice(a, a + P)


def build(nc, x_prompt, x_sample, cache_k, cache_v, state, vrows, bparams, rope, ada_w, w_in, w_out,
          w_router, w_gate, w_up, w_down, x_res, new_k, new_v, new_h):
    ctx = ExitStack()
    with ctx:
        def sb(name, shape, dt=F32):
            return ctx.enter_context(nc.sbuf_tensor(name, shape, dt))

        xn_dram = nc.dram_tensor("normed_rows", (TOK, D), F32, kind="Internal").ap()

        arena = sb("arena", [P, KD * IN_DIM + KD * D])
        RA = sb("RA", [P, NT * D])
        ident = sb("ident", [P, P])
        upto = sb("upto", [P, P])
        since = sb("since", [P, P])
        ones = sb("ones", [P, P])
        bars = sb("bars", [P, 2, P])
        ropes = sb("ropes", [P, NT, HD])
        vr = sb("vr", [P, P])
        vp = sb("vp", [P, VROWS])
        bp = sb("bp", [P, BCOLS])
        mod = sb("mod", [P, 48, 2])
        amp1 = sb("amp1", [P, KD, 2])
        amp2 = sb("amp2", [P, KD, 2])
        silc = sb("silc", [P, KD, 2])
        dtr = sb("dtr", [P, NT, 16])
        dt_ = sb("dt_", [P, NT, 16])
        adt = sb("adt", [P, NT, 16])
        dte = sb("dte", [P, NT, 16])
        dts = sb("dts", [P, NT, 16])
        negA = sb("negA", [P, 16])
        cs = sb("cs", [P, 4, NT, 8])
        ncs = sb("ncs", [P, 2, NT, 8])
        ecs = sb("ecs", [P, 2, NT, 8])
        wend = sb("wend", [P, 2, NT, 8])
        etot = sb("etot", [P, 2, NT, 8])
        cds = sb("cds", [P, 3, 2, GQ])
        ckv = sb("ckv", [P, 2, P])
        hst = sb("hst", [P, 2, 2, P])
        wr = sb("wr", [P, KD, EXP])
        ss = sb("ss", [P, 3, NT])
        rs = sb("rs", [P, 3, NT])
        hs = sb("hs", [P, NT, 10])
        mhalf = sb("mhalf", [P, NT * 10])
        nmax = sb("nmax", [P, 4])
        psum_ = sb("psum_", [P, 4])
        rinv = sb("rinv", [P, 4])
        aff = sb("aff", [P, NT, EXP])
        am = sb("am", [P, NT])
        top = sb("top", [P, 2, SLOT])
        topu = sb("topu", [EXP, SLOT], U32)
        col = sb("col", [SLOT, 2, EXP + 1])
        idx_g = sb("idx_g", [SLOT, 1], I32)
        idx_s = sb("idx_s", [SLOT, 1], I32)
        gcur = sb("gcur", [SLOT, 1])
        hold = sb("hold", [P, 1])
        pgate = sb("pgate", [P, 2])
        trunk = ExitStack()
        def tb(name, shape):
            return trunk.enter_context(nc.sbuf_tensor(name, shape, F32))

        RB = tb("RB", [P, KD * TOK])
        RC = tb("RC", [P, NT * D])
        RD = tb("RD", [P, NT * 256])
        RE = tb("RE", [P, NC_ * XL])
        RF = tb("RF", [P, NC_ * CL])
        trunk.close()
        wh = sb("wh", [P, 8, 1024], F32R)
        wl = sb("wl", [P, 8, 1024], F32R)
        xeh = sb("xeh", [P, KD, SLOT], F32R)
        xel = sb("xel", [P, KD, SLOT], F32R)
        hdh = sb("hdh", [P, KD, SLOT], F32R)
        hdl = sb("hdl", [P, KD, SLOT], F32R)
        PS = ctx.enter_context(nc.psum_tensor("PS", [P, 8 * 512], F32))

        def bank(b, n=512):
            return PS[:, b * 512:b * 512 + n]

        x_t = RA[:, :].rearrange("p (t d) -> p t d", t=NT)
        cat = x_t
        hT = RB[:, :].rearrange("p (j s) -> p j s", j=KD)
        q_t = RC[:, 0:NT * 512].rearrange("p (t c) -> p t c", t=NT)
        z_t = RC[:, NT * 512:].rearrange("p (t c) -> p t c", t=NT)
        xr = RC[:, :].rearrange("p (t d) -> p t d", t=NT)
        kv_t = RD[:, :].rearrange("p (t c) -> p t c", t=NT)
        xin = RE[:, :].rearrange("p (c s) -> p c s", c=NC_)
        cv = RF[:, :].rearrange("p (c s) -> p c s", c=NC_)
        tokx = RE[:, 0:NT * 640].rearrange("p (t c) -> p t c", t=NT)
        qT = RE[:, 0:GQ * TOK].rearrange("p (m s) -> p m s", m=GQ)
        kT = RE[:, GQ * TOK:GQ * TOK + 768]
        g1b = RE[:, 0:2 * D].rearrange("p (s d) -> p s d", s=2)
        junk = RE[:, 2 * D:3 * D]
        optmp = RF[:, 0:D]
        mrows = RF[:, D:D + 1536].rearrange("p (b c) -> p b c", b=3)
        hprev = RF[:, 0:2048].rearrange("p (s r c) -> p s r c", s=4, r=2)
        hctx = RF[:, 2048:2560].rearrange("p (r c) -> p r c", r=2)
        probs = RF[:, 0:1280].rearrange("p (i c) -> p i c", i=2)
        pT = RF[:, 1280:2560].rearrange("p (i c) -> p i c", i=2)
        EW = RB[:, 0:2048].rearrange("p (r c) -> p r c", r=2)
        xdt = RB[:, 2560:3584].rearrange("p (r c) -> p r c", r=2)
        xskip = RB[:, 3584:4608].rearrange("p (r c) -> p r c", r=2)
        ytmp = RB[:, 4608:5120]
        sqtmp = RF[:, 2048:2560]
        xw = [RB[:, 0:1024], RB[:, 1024:2048], RB[:, 2560:3584], RB[:, 3584:4608]]
        xg = RA[0:SLOT, 0:D]
        ys = RA[0:SLOT, D:2 * D]
        hid = RA[0:SLOT, 2 * D:3 * D]
        g2r = RA[0:SLOT, 3 * D:4 * D]
        wa = RE[0:EXP, 0:TOK]
        wb = RE[0:EXP, TOK:2 * TOK]

        primes = []

        class Signal:

            def __init__(self, name, per, unit=1, primed=False):
                self.sem = ctx.enter_context(nc.semaphore(name))
                self.per, self.unit = per, unit
                self.one = int(primed)
                if primed:
                    primes.append(self.sem)

            def at(self, l, n):
                return l * (self.per * self.unit) + (n * self.unit + self.one)

        class Chain:

            def __init__(self, eng, name, per):
                self.eng, self.name, self.per, self.n = eng, name, per, 0
                self.sem = ctx.enter_context(nc.semaphore(name))

            def start(self, rnd):
                self.rnd, self.n = rnd, 0

            def link(self, ins):
                self.n += 1
                ins.then_inc(self.sem, 1)
                self.eng.wait_ge(self.sem, self.rnd * self.per + self.n)

            def end(self):
                assert self.n == self.per, f"{self.name}: {self.n} links, {self.per} stated"

        dve_consts = ctx.enter_context(nc.semaphore("dve_consts"))
        pool_consts = ctx.enter_context(nc.semaphore("pool_consts"))
        rope_in = ctx.enter_context(nc.semaphore("rope_in"))
        x_copied = ctx.enter_context(nc.semaphore("x_copied"))
        vec_in = Signal("vec_in", 2, 16)
        x_in = Signal("x_in", 1, 16)
        x2_in = Signal("x2_in", 1, 16)
        ckv_in = Signal("ckv_in", 2, 16)
        h0_in = Signal("h0_in", 8, 16)
        wr_in = Signal("wr_in", 1, 16)
        ada_in = [Signal(f"ada_in{i}", 2, 16) for i in range(4)]
        win_in = [Signal(f"win_in{i}", 1, 16) for i in range(2)]
        wout_in = Signal("wout_in", 1, 16)
        ew_in = [Signal(f"ew_in{i}", EXP, 32) for i in range(6)]
        vec_ps = Signal("vec_ps", 1)
        vp_rdy = Signal("vp_rdy", 1)
        silc_rdy = Signal("silc_rdy", 1)
        ada_used = Signal("ada_used", 8)
        rows0 = Signal("rows0", 1)
        rows_act = Signal("rows_act", 1)
        rows_dve = Signal("rows_dve", 1)
        mod_ps = Signal("mod_ps", 1)
        mod_rdy = Signal("mod_rdy", 1)
        ss_rdy = Signal("ss_rdy", 15)
        u_rdy = Signal("u_rdy", 15)
        rstd_rdy = Signal("rstd_rdy", 15)
        xn_rdy = Signal("xn_rdy", 15)
        tg_ps = Signal("tg_ps", 30)
        tg_dve = Signal("tg_dve", 15)
        tg_act = Signal("tg_act", 15)
        ip_ps = Signal("ip_ps", 27)
        ip_ev = Signal("ip_ev", 27)
        pads = Signal("pads", 1)
        tap0 = Signal("tap0", NC_)
        conv_rdy = Signal("conv_rdy", NC_)
        xs_rdy = Signal("xs_rdy", NC_)
        dt_abs = Signal("dt_abs", 1)
        dt_e = Signal("dt_e", 1)
        a_rdy = Signal("a_rdy", 1)
        cs_ps = Signal("cs_ps", 1)
        cs_rdy = Signal("cs_rdy", 1)
        cs_e = Signal("cs_e", 1)
        wend_rdy = Signal("wend_rdy", 1)
        h0_ps = Signal("h0_ps", 1)
        tok_ps = Signal("tok_ps", NT)
        tok_ev = Signal("tok_ev", NT)
        xw_rdy = Signal("xw_rdy", 4)
        S_ps = Signal("S_ps", 4)
        h_rdy = Signal("h_rdy", 4)
        hf_ps = Signal("hf_ps", 1)
        hf_ev = Signal("hf_ev", 1)
        G_ps = Signal("G_ps", 2 * NT)
        seg_ps = Signal("seg_ps", 2 * NT)
        m_rdy = Signal("m_rdy", 2 * NT)
        e_rdy = Signal("e_rdy", 2 * NT)
        w_rdy = Signal("w_rdy", 2 * NT)
        xdt_rdy = Signal("xdt_rdy", 2 * NT)
        skip_rdy = Signal("skip_rdy", NT)
        yd_ps = Signal("yd_ps", 2 * NT)
        y_ps = Signal("y_ps", NT - 1)
        y_done = Signal("y_done", NT)
        k_rdy = Signal("k_rdy", 1)
        q_rdy = Signal("q_rdy", NT)
        qs_rdy = Signal("qs_rdy", 6)
        hsu_rdy = Signal("hsu_rdy", 1)
        hrs_rdy = Signal("hrs_rdy", 1)
        qkT_ps = Signal("qkT_ps", 6)
        qkT_act = Signal("qkT_act", 3)
        qkT_dve = Signal("qkT_dve", 3)
        UN = NT * HEADS
        s_ps = Signal("s_ps", UN)
        max_rdy = Signal("max_rdy", UN)
        p_rdy = Signal("p_rdy", UN)
        t_ps = Signal("t_ps", UN)
        pT_rdy = Signal("pT_rdy", UN)
        rinv_rdy = Signal("rinv_rdy", UN)
        o_ps = Signal("o_ps", UN)
        o_ev = Signal("o_ev", UN)
        g1_ps = Signal("g1_ps", 1)
        g1_rdy = Signal("g1_rdy", 1)
        op_ps = Signal("op_ps", NT)
        op_ev = Signal("op_ev", NT)
        x2_rdy = Signal("x2_rdy", NT)
        stored = Signal("stored", 2 * NT, 16)
        kv_out = Signal("kv_out", 2, 16)
        h_out = Signal("h_out", 8, 16, primed=True)
        lg_ps = Signal("lg_ps", 1)
        lg_sub = Signal("lg_sub", 1)
        lg_e = Signal("lg_e", 1)
        aff_rdy = Signal("aff_rdy", 1)
        affT_ps = Signal("affT_ps", 1)
        top_rdy = Signal("top_rdy", 1)
        col_ps = Signal("col_ps", 1)
        col_rdy = Signal("col_rdy", 1)
        idx_rdy = Signal("idx_rdy", EXP + 1)
        idxs_rdy = Signal("idxs_rdy", EXP)
        held = Signal("held", 2 * EXP + 1, primed=True)
        gathered = Signal("gathered", EXP + 1, 16)
        scattered = Signal("scattered", EXP, 16)
        landed = Signal("landed", EXP, primed=True)
        xT_ps = Signal("xT_ps", EXP)
        xm_rdy = Signal("xm_rdy", EXP)
        xh_rdy = Signal("xh_rdy", EXP)
        xl_rdy = Signal("xl_rdy", EXP)
        hi_rdy = Signal("hi_rdy", 24 * EXP)
        lo_dve = Signal("lo_dve", 3 * EXP * len(DVE_SLABS), primed=True)
        lo_pool = Signal("lo_pool", 3 * EXP * len(POOL_SLABS), primed=True)
        slab_used = Signal("slab_used", 24 * EXP)
        sg_rdy = Signal("sg_rdy", 2 * EXP)
        hm_rdy = Signal("hm_rdy", 2 * EXP)
        ht_ps = Signal("ht_ps", 2 * EXP)
        hh_rdy = Signal("hh_rdy", 2 * EXP)
        hl_rdy = Signal("hl_rdy", 2 * EXP)
        d_ev = Signal("d_ev", EXP, primed=True)
        ys_rdy = Signal("ys_rdy", EXP)
        g2_ps = Signal("g2_ps", 1)
        g2_rdy = Signal("g2_rdy", 1)

        def slab(j, i):
            half, w = i // 4, i % 4
            a = arena[:, (2 * j + half) * 4096 + w * SLAB:(2 * j + half) * 4096 + (w + 1) * SLAB]
            a = a.rearrange("p (k n) -> p k n", n=512)
            return a, ((half, 2 * w), (half, 2 * w + 1)) if j < 2 else ((0, i), (1, i))

        def slabs_of(i):
            return (lo_dve, DVE_SLABS) if i in DVE_SLABS else (lo_pool, POOL_SLABS)

        def lo_value(E, j, i):
            sig, mine = slabs_of(i)
            return E * (3 * len(mine)) + (len(mine) * j + mine.index(i) + 2)

        def two(a):
            return a.rearrange("p (k n) -> p k n", n=512)

        block = ctx.enter_context(nc.Block())

        def each_layer(eng):
            return eng.Fori(0, LAYERS)

        F_STEP = (0, 1, 2, 3)
        B_STEP = (0, 4, 3, 2)

        @block.sync
        def _(sp):
            sp.dma_start(x_res[0:CTX, :], x_prompt).then_inc(x_copied, 16)
            sp.dma_start(x_res[CTX:TOK, :], x_sample).then_inc(x_copied, 16)
            sp.dma_start(ropes[:, :, :], rope).then_inc(rope_in, 16)
            with each_layer(sp) as l:
                row = lambda a: a[bass.ds(l, 1)]
                sp.wait_ge(lo_dve.sem, lo_dve.at(l, 0))
                sp.dma_start(vr[0:VROWS, :], row(vrows).rearrange("a r c -> (a r) c")).then_inc(vec_in.sem, 16)
                sp.dma_start(bp[:, :], row(bparams).to_broadcast([P, BCOLS])).then_inc(vec_in.sem, 16)
                sp.dma_start(ckv[:, 0, :], row(cache_k).rearrange("a s c -> (a s) c")).then_inc(ckv_in.sem, 16)
                sp.dma_start(ckv[:, 1, :], row(cache_v).rearrange("a s c -> (a s) c")).then_inc(ckv_in.sem, 16)
                sp.dma_start(wr[:, :, :], row(w_router).rearrange("a (k p) e -> p (a k) e", p=P)).then_inc(wr_in.sem, 16)
                sp.wait_ge(h_out.sem, h_out.at(l, 0))
                for r in range(2):
                    for m in range(2):
                        for g in range(2):
                            h = g * GQ + 2 * m
                            src = row(state)[:, r, h:h + 2].rearrange("a h p n -> (a h p) n")
                            sp.dma_start(hst[:, r, m, g * HD:(g + 1) * HD], src).then_inc(h0_in.sem, 16)
                for c in range(8):
                    i = c % 4
                    if c < 4:
                        sp.wait_ge(lo_dve.sem, lo_dve.at(l, 0))
                        sp.wait_ge(lo_pool.sem, lo_pool.at(l, 0))
                    else:
                        sp.wait_ge(ada_used.sem, ada_used.at(l, c - 3))
                    sp.dma_start(arena[:, i * 6144:(i + 1) * 6144],
                                 row(ada_w)[:, c * P:(c + 1) * P, :].rearrange("a p n -> (a p) n")
                                 ).then_inc(ada_in[i].sem, 16)
                for hlf in range(2):
                    sp.wait_ge(ada_used.sem, ada_used.at(l, 6 + hlf))
                    k0 = hlf * 4
                    sp.dma_start(arena[:, k0 * IN_DIM:(k0 + 4) * IN_DIM].rearrange("p (k n) -> p k n", k=4),
                                 row(w_in)[:, k0 * P:(k0 + 4) * P, :].rearrange("a (k p) n -> p (a k) n", p=P)
                                 ).then_inc(win_in[hlf].sem, 16)
                sp.wait_ge(ada_used.sem, ada_used.at(l, 8))
                sp.dma_start(arena[:, KD * IN_DIM:].rearrange("p (k n) -> p k n", k=KD),
                             row(w_out).rearrange("a (k p) n -> p (a k) n", p=P)).then_inc(wout_in.sem, 16)
                def expert_part(E, j, mine):
                    slabs = [i for i in mine if i // 4 == j % 2]
                    s0, n = slabs[0], len(slabs)
                    place = arena[:, j * 4096 + s0 % 4 * SLAB:j * 4096 + (s0 % 4 + n) * SLAB]
                    if j < 4:
                        k0 = s0 % 4 * 2 * P
                        w = (w_gate, w_up)[j // 2][bass.ds(E, 1), k0:k0 + 2 * n * P,
                                                   (j % 2) * 512:(j % 2 + 1) * 512]
                        place = place.rearrange("p (k n) -> p k n", n=512)
                    else:
                        w = w_down[bass.ds(E, 1), s0 * P:(s0 + n) * P, :]
                        place = place.rearrange("p (k n) -> p k n", n=1024)
                    sp.dma_start(place, w.rearrange("a (k p) n -> p (a k) n", p=P)).then_inc(ew_in[j].sem, 16)

                for j in range(6):
                    if j == 0:
                        sp.wait_ge(ip_ps.sem, ip_ps.at(l, 27))
                    elif j == 4:
                        sp.wait_ge(op_ps.sem, op_ps.at(l, NT))
                    expert_part(l * EXP, j, DVE_SLABS)
                    expert_part(l * EXP, j, POOL_SLABS)
                with sp.Fori(1, EXP) as e:
                    for j in range(6):
                        for mine in (DVE_SLABS, POOL_SLABS):
                            last = max(i for i in mine if i // 4 <= j % 2)
                            sp.wait_ge(slabs_of(last)[0].sem, lo_value(l * EXP + e - 1, j // 2, last))
                            expert_part(l * EXP + e, j, mine)
            sp.wait_ge(x_copied, 32)
            sp.wait_ge(stored.sem, stored.at(LAYERS, 0))
            sp.wait_ge(kv_out.sem, kv_out.at(LAYERS, 0))
            sp.wait_ge(h_out.sem, h_out.at(LAYERS, 0))
            sp.wait_ge(landed.sem, landed.at(LAYERS, 0))

        @block.tensor
        def _(pe):
            mm = nc.tensor.matmul

            def transpose_groups(l, use, src, base):
                last = None
                for g in range(10):
                    if g >= 8:
                        s = (tg_dve, tg_act)[g % 2]
                        pe.wait_ge(s.sem, s.at(l, use * 5 + 1))
                    b = bank((base + g) % 8)
                    for i in range(4):
                        t, j = (1 + i, g) if g < 8 else (0, (g - 8) * 4 + i)
                        if g == 0:
                            pe.wait_ge(xn_rdy.sem, xn_rdy.at(l, use * NT + t + 1))
                        last = nc.tensor.transpose(b[:, i * P:(i + 1) * P], src[:, t, j * P:(j + 1) * P], ident[:, :])
                    last.then_inc(tg_ps.sem, 1)

            def transposed(l, use):
                pe.wait_ge(tg_dve.sem, tg_dve.at(l, use * 5 + 5))
                pe.wait_ge(tg_act.sem, tg_act.at(l, use * 5 + 5))

            def product(E, j, i):
                _, parts = slab(j, i)
                th, tl = (hdh, hdl) if j == 2 else (xeh, xel)
                pe.wait_ge(slabs_of(i)[0].sem, lo_value(E, j, i))
                for part, (n, k) in enumerate(parts):
                    o = (2 * j + n) * 512
                    for p_, (tok, wgt) in enumerate(((th, wh), (th, wl), (tl, wh))):
                        last = mm(PS[0:SLOT, o:o + 512], tok[:, k, :], two(wgt[:, i, :])[:, part, :],
                                  start=(k == 0 and p_ == 0), stop=(k == KD - 1 and p_ == 2), skip_group_check=True)
                last.then_inc(slab_used.sem, 1)

            def tokens_in(l, E):
                pe.wait_ge(gathered.sem, E * 16 + l * 16 + 16)
                for j in range(8):
                    o = (6 + j // 4) * 512 + (j % 4) * SLOT
                    last = nc.tensor.transpose(PS[:, o:o + SLOT], xg[:, j * P:(j + 1) * P], ident[0:SLOT, 0:SLOT])
                last.then_inc(xT_ps.sem, 1)

            def hidden(E, n):
                pe.wait_ge(hm_rdy.sem, 2 * E + (n + 1))
                for j in range(4):
                    o = (2 + n) * 512 + j * SLOT
                    last = nc.tensor.transpose(PS[:, o:o + SLOT], hid[:, (4 * n + j) * P:(4 * n + j + 1) * P], ident[0:SLOT, 0:SLOT])
                last.then_inc(ht_ps.sem, 1)

            def down(E):
                pe.wait_ge(d_ev.sem, E + 1)
                for i in range(8):
                    if i == 3:
                        hidden(E, 1)
                    if i % 4 == 0:
                        pe.wait_ge(hl_rdy.sem, 2 * E + (i // 4 + 1))
                    product(E, 2, i)

            def gate_up(E):
                pe.wait_ge(xl_rdy.sem, E + 1)
                for i in range(8):
                    product(E, 0, i)
                for i in range(8):
                    product(E, 1, i)
                    if i == 5:
                        hidden(E, 0)

            pe.wait_ge(dve_consts, 4)
            pe.wait_ge(pool_consts, 8)
            with each_layer(pe) as l:
                pe.wait_ge(vec_in.sem, vec_in.at(l, 2))
                nc.tensor.transpose(bank(0, VROWS), vr[0:VROWS, :], ident[0:VROWS, 0:VROWS]).then_inc(vec_ps.sem, 1)
                pe.wait_ge(silc_rdy.sem, silc_rdy.at(l, 1))
                last = None
                for c in range(8):
                    i = c % 4
                    pe.wait_ge(ada_in[i].sem, ada_in[i].at(l, c // 4 + 1))
                    for b in range(3):
                        for q in range(4):
                            a = i * 6144 + (4 * b + q) * 512
                            last = mm(PS[32 * q:32 * q + 2, (1 + b) * 512:(2 + b) * 512], silc[:, c, :], arena[:, a:a + 512],
                                      start=(c == 0), stop=(c == 7), skip_group_check=True)
                    last.then_inc(ada_used.sem, 1)
                pe.wait_ge(rows_act.sem, rows_act.at(l, 1))
                pe.wait_ge(rows_dve.sem, rows_dve.at(l, 1))
                for b in range(3):
                    for i in range(4):
                        o = (4 + b) * 512 + i * P
                        last = nc.tensor.transpose(PS[:, o:o + P], mrows[:, b, i * P:(i + 1) * P], ident[:, :])
                last.then_inc(mod_ps.sem, 1)
                pe.wait_ge(mod_rdy.sem, mod_rdy.at(l, 1))
                transpose_groups(l, 0, x_t, 0)
                transposed(l, 0)

                pe.wait_ge(win_in[0].sem, win_in[0].at(l, 1))
                n = 0

                def project(parts):
                    nonlocal n
                    if n >= 8:
                        pe.wait_ge(ip_ev.sem, ip_ev.at(l, n - 7))
                    last = None
                    for o, wdt, lhs, rhs in parts:
                        for k in range(KD):
                            if n == 0 and k == 4:
                                pe.wait_ge(win_in[1].sem, win_in[1].at(l, 1))
                            last = mm(PS[:, (n % 8) * 512 + o:(n % 8) * 512 + o + wdt], lhs(k), rhs(k),
                                      start=(k == 0), stop=(k == KD - 1))
                    last.then_inc(ip_ps.sem, 1)
                    n += 1

                wcol = lambda k, a, w: arena[:, k * IN_DIM + a:k * IN_DIM + a + w]
                for c in range(NC_):
                    for _, s0, sn in (SETS[1], SETS[0]):
                        project([(0, sn, lambda k: wcol(k, C_XBC + c * P, P), lambda k: hT[:, k, s0:s0 + sn])])
                tokens = lambda t: (lambda k: hT[:, k, t * P:(t + 1) * P])
                for t in range(NT):
                    project([(0, 256, tokens(t), lambda k: wcol(k, C_KV, 256)),
                             (256, 16, tokens(t), lambda k: wcol(k, C_DT, 16))])
                for t in range(NT):
                    project([(0, 512, tokens(t), lambda k: wcol(k, C_Q, 512))])
                for t in range(NT):
                    project([(0, 512, tokens(t), lambda k: wcol(k, C_Z, 512))])

                pe.wait_ge(ip_ev.sem, ip_ev.at(l, 27))
                pe.wait_ge(a_rdy.sem, a_rdy.at(l, 1))
                mm(PS[:, 0:40], upto[:, :], adt[:, :, 0:8], start=True, stop=True)
                mm(PS[:, 40:80], since[:, :], adt[:, :, 8:16], start=True, stop=True)
                mm(PS[:, 80:120], ones[:, :], adt[:, :, 0:8], start=True, stop=True)
                mm(PS[:, 120:160], ones[:, :], adt[:, :, 8:16], start=True, stop=True).then_inc(cs_ps.sem, 1)
                pe.wait_ge(h0_in.sem, h0_in.at(l, 8))
                for r in range(2):
                    for m in range(2):
                        last = nc.tensor.transpose(PS[:, 512 + (2 * r + m) * P:512 + (2 * r + m + 1) * P],
                                                   hst[:, r, m, :], ident[:, :])
                last.then_inc(h0_ps.sem, 1)
                pe.wait_ge(xs_rdy.sem, xs_rdy.at(l, NC_))
                for t in range(NT):
                    b = 2 + 2 * (t % 3)
                    if t >= 3:
                        pe.wait_ge(tok_ev.sem, tok_ev.at(l, t - 2))
                    for c in range(5):
                        last = nc.tensor.transpose(PS[:, b * 512 + c * P:b * 512 + (c + 1) * P],
                                                   cv[:, c, conv_cols(t)], ident[:, :])
                    last.then_inc(tok_ps.sem, 1)
                pe.wait_ge(tok_ev.sem, tok_ev.at(l, NT))

                for s in range(4):
                    pe.wait_ge(xw_rdy.sem, xw_rdy.at(l, s + 1))
                    for r, t in ((0, F_STEP[s]), (1, B_STEP[s])):
                        for g in range(2):
                            o = (4 + s) * 512 + r * 256
                            last = mm(PS[g * HD:(g + 1) * HD, o:o + 256], tokx[:, t, 512 + g * HD:512 + (g + 1) * HD],
                                      xw[s][:, r * 512 + g * 256:r * 512 + (g + 1) * 256], start=True, stop=True)
                    last.then_inc(S_ps.sem, 1)

                def scores(t):
                    for g in range(2):
                        if t or g:
                            pe.wait_ge(G_ps.sem, G_ps.at(l, 2 * t + g))
                        mm(PS[:, g * P:(g + 1) * P], cv[g * HD:(g + 1) * HD, 4, conv_cols(t)],
                           cv[g * HD:(g + 1) * HD, 5, conv_cols(t)], start=True, stop=True).then_inc(G_ps.sem, 1)

                def cumulated(t):
                    for r in range(2):
                        if t:
                            pe.wait_ge(m_rdy.sem, m_rdy.at(l, 2 * (t - 1) + r + 1))
                        for h in range(8):
                            o = (2 + 2 * r) * 512 + h * P
                            last = nc.tensor.transpose(PS[:, o:o + P], cs[:, r, t, h:h + 1].to_broadcast([P, P]), ident[:, :])
                        last.then_inc(seg_ps.sem, 1)

                pe.wait_ge(h_rdy.sem, h_rdy.at(l, 4))
                cumulated(0)
                scores(0)
                for t in range(NT):
                    if t + 1 < NT:
                        cumulated(t + 1)
                    if t:
                        pe.wait_ge(y_done.sem, y_done.at(l, t))
                    for r in range(2):
                        pe.wait_ge(w_rdy.sem, w_rdy.at(l, 2 * t + r + 1))
                        pe.wait_ge(xdt_rdy.sem, xdt_rdy.at(l, 2 * t + r + 1))
                        for h in range(8):
                            last = mm(PS[:, 512 + h * HD:512 + (h + 1) * HD], EW[:, r, h * P:(h + 1) * P],
                                      xdt[:, r, h * HD:(h + 1) * HD], start=(r == 0 and h == 0), stop=(r == 1),
                                      skip_group_check=True)
                        last.then_inc(yd_ps.sem, 1)
                    if t + 1 < NT:
                        scores(t + 1)
                    if t:
                        for r, s in ((0, t - 1), (1, 4 - t)):
                            for g in range(2):
                                last = mm(PS[:, (6 + g) * 512 + r * 256:(6 + g) * 512 + (r + 1) * 256],
                                          cv[g * HD:(g + 1) * HD, 5, conv_cols(t)],
                                          hprev[g * HD:(g + 1) * HD, s, r, :], start=True, stop=True)
                        last.then_inc(y_ps.sem, 1)
                    else:
                        for r in range(2):
                            for m in range(2):
                                last = nc.tensor.transpose(PS[:, 3072 + (2 * r + m) * P:3072 + (2 * r + m + 1) * P],
                                                           hctx[:, r, m * P:(m + 1) * P], ident[:, :])
                        last.then_inc(hf_ps.sem, 1)
                        pe.wait_ge(hf_ev.sem, hf_ev.at(l, 1))

                pe.wait_ge(y_done.sem, y_done.at(l, NT))
                pe.wait_ge(k_rdy.sem, k_rdy.at(l, 1))
                pe.wait_ge(ckv_in.sem, ckv_in.at(l, 2))
                for i in range(6):
                    src = ckv[:, 0, :] if i == 1 else kv_t[:, (0, 0, 1, 2, 3, 4)[i], 0:P]
                    last = nc.tensor.transpose(PS[:, i * P:(i + 1) * P], src, ident[:, :])
                last.then_inc(qkT_ps.sem, 1)
                for t in range(NT):
                    pe.wait_ge(q_rdy.sem, q_rdy.at(l, t + 1))
                    for m in range(GQ):
                        o = (2 + t) * 512 + m * P
                        last = nc.tensor.transpose(PS[:, o:o + P], q_t[:, t, m * P:(m + 1) * P], ident[:, :])
                    last.then_inc(qkT_ps.sem, 1)
                pe.wait_ge(qkT_act.sem, qkT_act.at(l, 3))
                pe.wait_ge(qkT_dve.sem, qkT_dve.at(l, 3))

                def qk(u):
                    t, h = u // HEADS, u % HEADS
                    g, m = h // GQ, h % GQ
                    if u >= 2:
                        pe.wait_ge(p_rdy.sem, p_rdy.at(l, u - 1))
                    o = (u % 2) * 1024
                    for a, n_, k0 in (((0, 512, P), (512, 128, P + 512)) if t else ((0, P, 0),)):
                        last = mm(PS[:, o + a:o + a + n_], qT[g * HD:(g + 1) * HD, m, t * P:(t + 1) * P],
                                  kT[g * HD:(g + 1) * HD, k0:k0 + n_], start=True, stop=True)
                    last.then_inc(s_ps.sem, 1)

                qk(0)
                qk(1)
                for u in range(UN):
                    t, h = u // HEADS, u % HEADS
                    g = h // GQ
                    tiles = range(5 if t else 1)
                    pe.wait_ge(p_rdy.sem, p_rdy.at(l, u + 1))
                    if u:
                        pe.wait_ge(pT_rdy.sem, pT_rdy.at(l, u))
                    for i in tiles:
                        last = nc.tensor.transpose(PS[:, 2048 + i * P:2048 + (i + 1) * P],
                                                   probs[:, u % 2, i * P:(i + 1) * P], ident[:, :])
                    last.then_inc(t_ps.sem, 1)
                    if u + 2 < UN:
                        qk(u + 2)
                    pe.wait_ge(pT_rdy.sem, pT_rdy.at(l, u + 1))
                    if u >= 2:
                        pe.wait_ge(o_ev.sem, o_ev.at(l, u - 1))
                    for i in tiles:
                        v = (ckv[:, 1, :] if i == 0 else kv_t[:, i, P:2 * P]) if t else kv_t[:, 0, P:2 * P]
                        o = (6 + u % 2) * 512
                        last = mm(PS[:, o:o + HD], pT[:, u % 2, i * P:(i + 1) * P], v[:, g * HD:(g + 1) * HD],
                                  start=(i == 0), stop=(i == len(tiles) - 1))
                    last.then_inc(o_ps.sem, 1)

                pe.wait_ge(o_ev.sem, o_ev.at(l, UN))
                for s in range(2):
                    for j in range(KD):
                        o = (s * KD + j) * P
                        last = nc.tensor.transpose(PS[:, o:o + P], mod[:, 16 + j, s:s + 1].to_broadcast([P, P]), ident[:, :])
                last.then_inc(g1_ps.sem, 1)
                pe.wait_ge(g1_rdy.sem, g1_rdy.at(l, 1))
                transpose_groups(l, 1, cat, 4)
                transposed(l, 1)

                pe.wait_ge(wout_in.sem, wout_in.at(l, 1))
                for t in range(NT):
                    if t == 4:
                        pe.wait_ge(op_ev.sem, op_ev.at(l, 1))
                    for hlf in range(2):
                        for k in range(KD):
                            o = (t % 4) * 1024 + hlf * 512
                            w = KD * IN_DIM + k * D + hlf * 512
                            last = mm(PS[:, o:o + 512], hT[:, k, t * P:(t + 1) * P], arena[:, w:w + 512],
                                      start=(k == 0), stop=(k == KD - 1))
                    last.then_inc(op_ps.sem, 1)

                pe.wait_ge(op_ev.sem, op_ev.at(l, NT))
                transpose_groups(l, 2, x_t, 0)
                transposed(l, 2)
                pe.wait_ge(wr_in.sem, wr_in.at(l, 1))
                for t in range(NT):
                    for k in range(KD):
                        last = mm(PS[:, 1024 + t * EXP:1024 + (t + 1) * EXP], hT[:, k, t * P:(t + 1) * P], wr[:, k, :],
                                  start=(k == 0), stop=(k == KD - 1))
                last.then_inc(lg_ps.sem, 1)
                pe.wait_ge(aff_rdy.sem, aff_rdy.at(l, 1))
                for t in range(NT):
                    last = nc.tensor.transpose(PS[0:EXP, 2048 + t * P:2048 + (t + 1) * P], aff[:, t, :], ident[:, :])
                last.then_inc(affT_ps.sem, 1)
                pe.wait_ge(top_rdy.sem, top_rdy.at(l, 1))
                for i in range(2):
                    last = nc.tensor.transpose(PS[0:SLOT, 3072 + i * P:3072 + (i + 1) * P], top[:, i, :], ident[:, :])
                last.then_inc(col_ps.sem, 1)

                for s in range(2):
                    for j in range(KD):
                        o = (s * KD + j) * P
                        last = nc.tensor.transpose(PS[:, o:o + P], mod[:, 40 + j, s:s + 1].to_broadcast([P, P]), ident[:, :])
                last.then_inc(g2_ps.sem, 1)
                pe.wait_ge(col_rdy.sem, col_rdy.at(l, 1))
                pe.wait_ge(g2_rdy.sem, g2_rdy.at(l, 1))
                tokens_in(l, l * EXP)
                gate_up(l * EXP)
                with pe.Fori(1, EXP) as e:
                    E = l * EXP + e
                    tokens_in(l, E)
                    down(E - 1)
                    gate_up(E)
                down(l * EXP + EXP - 1)
                pe.wait_ge(d_ev.sem, d_ev.at(l, EXP))

        @block.scalar
        def _(act):
            A = nc.scalar.activation

            def squares(l, use, t, src, out):
                if t:
                    act.wait_ge(ss_rdy.sem, ss_rdy.at(l, use * NT + t))
                A(out, src, ACT.Square, accum_out=ss[:, use, t:t + 1]).then_inc(ss_rdy.sem, 1)

            def move_groups(l, use, amp, shift):
                for g in range(1, 10, 2):
                    act.wait_ge(tg_ps.sem, tg_ps.at(l, use * 10 + g + 1))
                    b = bank(((0, 4, 0)[use] + g) % 8)
                    if g < 8:
                        put(hT[:, g, CTX:TOK], b, amp(g, 1), shift(g, 1)).then_inc(tg_act.sem, 1)
                    else:
                        for i in range(4):
                            last = put(hT[:, 4 + i, 0:CTX], b[:, i * P:(i + 1) * P], amp(4 + i, 0), shift(4 + i, 0))
                        last.then_inc(tg_act.sem, 1)

            def put(out, in_, a, s):
                if a is None:
                    return A(out, in_, ACT.Copy)
                if s is None:
                    return A(out, in_, ACT.Copy, scale=a)
                return A(out, in_, ACT.Identity, scale=a, bias=s)

            def rounded(E, j, i, fresh=False):
                src, _ = slab(j, i)
                if i % 4 == 0:
                    act.wait_ge(ew_in[2 * j + i // 4].sem, E * 32 + 32)
                if not fresh:
                    act.wait_ge(slab_used.sem, 24 * E + (8 * j + i - 7))
                A(two(wh[:, i, :]), src, ACT.Copy).then_inc(hi_rdy.sem, 1)

            def tokens_high(E):
                act.wait_ge(xm_rdy.sem, E + 1)
                A(xeh[:, :, :].rearrange("p (b j) s -> p b (j s)", b=2),
                  PS[:, 3072:4096].rearrange("p (b c) -> p b c", b=2)[:, :, 0:320], ACT.Copy).then_inc(xh_rdy.sem, 1)

            def silu_gate(E, n):
                act.wait_ge(slab_used.sem, 24 * E + (4 * n + 4))
                A(hid[:, n * 512:(n + 1) * 512], PS[0:SLOT, n * 512:(n + 1) * 512], ACT.Silu).then_inc(sg_rdy.sem, 1)

            def hidden_high(E, n):
                act.wait_ge(ht_ps.sem, 2 * E + (n + 1))
                A(hdh[:, 4 * n:4 * n + 4, :].rearrange("p j s -> p (j s)"), PS[:, (2 + n) * 512:(2 + n) * 512 + 320],
                  ACT.Copy).then_inc(hh_rdy.sem, 1)

            def rows_out(E):
                act.wait_ge(slab_used.sem, 24 * E + 24)
                act.wait_ge(idxs_rdy.sem, E + 1)
                act.wait_ge(landed.sem, E + 1)
                A(ys, PS[0:SLOT, 2048:3072], ACT.Copy, scale=gcur[:, 0:1]).then_inc(d_ev.sem, 1)

            def act_down(E, at):
                for i in range(8):
                    rounded(E, 2, i)
                    if i == 1:
                        hidden_high(E, 0)
                    if i in at:
                        at[i]()
                    if i == 6:
                        hidden_high(E, 1)

            def act_gate_up(E, fresh, at):
                for i in range(16):
                    rounded(E, i // 8, i % 8, fresh and i < 8)
                    if i in at:
                        at[i]()
                    if i == 7:
                        silu_gate(E, 0)
                    if i == 11:
                        silu_gate(E, 1)

            act.wait_ge(x_copied, 32)
            with each_layer(act) as l:
                act.wait_ge(landed.sem, landed.at(l, 0))
                act.dma_start(x_t, x_res.rearrange("(t p) d -> p t d", p=P)).then_inc(x_in.sem, 16)
                act.wait_ge(vp_rdy.sem, vp_rdy.at(l, 1))
                A(silc[:, :, :].rearrange("p k s -> p s k"), vp[:, R_C:R_C + 16].rearrange("p (s k) -> p s k", s=2),
                  ACT.Silu).then_inc(silc_rdy.sem, 1)
                act.wait_ge(x_in.sem, x_in.at(l, 1))
                for t in range(NT):
                    squares(l, 0, t, x_t[:, t, :], optmp)
                act.wait_ge(ada_used.sem, ada_used.at(l, 8))
                act.wait_ge(rows0.sem, rows0.at(l, 1))
                for q in (0, 1):
                    last = A(mrows[32 * q:32 * q + 2, :, :], PS[32 * q:32 * q + 2, 512:2048].rearrange("p (b c) -> p b c", b=3), ACT.Copy)
                last.then_inc(rows_act.sem, 1)
                act.wait_ge(mod_rdy.sem, mod_rdy.at(l, 1))
                move_groups(l, 0, lambda j, s: amp1[:, j, s:s + 1], lambda j, s: mod[:, j, s:s + 1])

                act.wait_ge(pads.sem, pads.at(l, 1))
                n = 0

                def evac(out, in_):
                    nonlocal n
                    act.wait_ge(ip_ps.sem, ip_ps.at(l, n + 1))
                    A(out, in_, ACT.Copy).then_inc(ip_ev.sem, 1)
                    n += 1

                def conv_silu(c):
                    act.wait_ge(conv_rdy.sem, conv_rdy.at(l, c + 1))
                    A(cv[:, c, :], cv[:, c, :], ACT.Silu).then_inc(xs_rdy.sem, 1)

                for c in range(NC_):
                    evac(xin[:, c, CW + 2:CW + 2 + LAT], bank(n % 8))
                    evac(xin[:, c, 2:2 + CTX], bank(n % 8, CTX))
                    act.wait_ge(ip_ev.sem, ip_ev.at(l, n))
                    A(cv[:, c, :], xin[:, c, 0:CL], ACT.Identity, scale=vp[:, R_CW + c:R_CW + c + 1],
                      bias=vp[:, R_CB + c:R_CB + c + 1]).then_inc(tap0.sem, 1)
                    if c:
                        conv_silu(c - 1)
                for t in range(NT):
                    b = bank(n % 8)
                    act.wait_ge(ip_ps.sem, ip_ps.at(l, n + 1))
                    A(kv_t[:, t, :], b[:, 0:256], ACT.Copy)
                    A(dtr[:, t, :], b[:, 256:272], ACT.Copy).then_inc(ip_ev.sem, 1)
                    n += 1
                conv_silu(NC_ - 1)
                for t in range(NT):
                    b = bank(n % 8)
                    act.wait_ge(ip_ps.sem, ip_ps.at(l, n + 1))
                    A(q_t[:, t, :].rearrange("p (m g d) -> p g m d", m=GQ, g=KVH),
                      b.rearrange("p (g m d) -> p g m d", g=KVH, m=GQ), ACT.Copy).then_inc(ip_ev.sem, 1)
                    n += 1
                for t in range(NT):
                    act.wait_ge(ip_ps.sem, ip_ps.at(l, n + 1))
                    A(z_t[:, t, :], bank(n % 8), ACT.Silu).then_inc(ip_ev.sem, 1)
                    n += 1
                A(negA[:, :], bp[:, B_AL:B_AL + 16], ACT.Exp)
                act.wait_ge(dt_abs.sem, dt_abs.at(l, 1))
                A(dte[:, :, :], dts[:, :, :], ACT.Exp, scale=-1.0).then_inc(dt_e.sem, 1)
                act.wait_ge(cs_rdy.sem, cs_rdy.at(l, 1))
                A(ecs[:, :, :, :], cs[:, 0:2, :, :], ACT.Exp)
                A(etot[:, :, :, :], cs[:, 2:4, :, :], ACT.Exp)
                A(wend[:, :, :, :], wend[:, :, :, :], ACT.Exp).then_inc(cs_e.sem, 1)
                for t in range(NT):
                    act.wait_ge(tok_ps.sem, tok_ps.at(l, t + 1))
                    b = 2 + 2 * (t % 3)
                    A(tokx[:, t, :], PS[:, b * 512:b * 512 + 640], ACT.Copy).then_inc(tok_ev.sem, 1)
                for t in range(NT):
                    for r in range(2):
                        act.wait_ge(m_rdy.sem, m_rdy.at(l, 2 * t + r + 1))
                        A(EW[:, r, :], EW[:, r, :], ACT.Exp).then_inc(e_rdy.sem, 1)
                    if t == 0:
                        act.wait_ge(hf_ps.sem, hf_ps.at(l, 1))
                        act.wait_ge(h0_ps.sem, h0_ps.at(l, 1))
                        A(hst[:, :, :, :].rearrange("p r m c -> p (r m c)"), bank(6), ACT.Copy).then_inc(hf_ev.sem, 1)
                    if t:
                        act.wait_ge(y_done.sem, y_done.at(l, t))
                        squares(l, 1, t - 1, cat[:, t - 1, 512:1024], sqtmp)
                act.wait_ge(y_done.sem, y_done.at(l, NT))
                squares(l, 1, NT - 1, cat[:, NT - 1, 512:1024], sqtmp)
                act.wait_ge(hf_ev.sem, hf_ev.at(l, 1))
                for r in range(2):
                    for m in range(2):
                        for g in range(2):
                            h = g * GQ + 2 * m
                            dst = new_h[bass.ds(l, 1), r, h:h + 2].rearrange("a h p n -> (a h p) n")
                            act.dma_start(dst, hst[:, r, m, g * HD:(g + 1) * HD]).then_inc(h_out.sem, 16)
                act.wait_ge(k_rdy.sem, k_rdy.at(l, 1))
                act.dma_start(new_k[bass.ds(l, 1)].rearrange("a s c -> (a s) c"), kv_t[:, 0, 0:P]).then_inc(kv_out.sem, 16)
                act.dma_start(new_v[bass.ds(l, 1)].rearrange("a s c -> (a s) c"), kv_t[:, 0, P:2 * P]).then_inc(kv_out.sem, 16)
                act.wait_ge(qkT_ps.sem, qkT_ps.at(l, 1))
                A(kT, PS[:, 0:768], ACT.Copy).then_inc(qkT_act.sem, 1)
                for t in (3, 4):
                    act.wait_ge(qkT_ps.sem, qkT_ps.at(l, t + 2))
                    A(qT[:, :, t * P:(t + 1) * P], bank(2 + t).rearrange("p (m s) -> p m s", m=GQ), ACT.Copy).then_inc(qkT_act.sem, 1)
                act.wait_ge(qkT_ps.sem, qkT_ps.at(l, 6))
                act.wait_ge(y_done.sem, y_done.at(l, NT))
                act.dma_start(xr, x_res.rearrange("(t p) d -> p t d", p=P)).then_inc(x2_in.sem, 16)
                for u in range(UN + 2):
                    if u < UN:
                        n_ = 640 if u >= HEADS else P
                        act.wait_ge(max_rdy.sem, max_rdy.at(l, u + 1))
                        if u >= 2:
                            act.wait_ge(t_ps.sem, t_ps.at(l, u - 1))
                        if u >= 4:
                            act.wait_ge(rinv_rdy.sem, rinv_rdy.at(l, u - 3))
                        A(probs[:, u % 2, 0:n_], PS[:, (u % 2) * 1024:(u % 2) * 1024 + n_], ACT.Exp,
                          bias=nmax[:, u % 4:u % 4 + 1], accum_out=psum_[:, u % 4:u % 4 + 1]).then_inc(p_rdy.sem, 1)
                    if u >= 2:
                        v = u - 2
                        t, h = v // HEADS, v % HEADS
                        act.wait_ge(o_ps.sem, o_ps.at(l, v + 1))
                        act.wait_ge(rinv_rdy.sem, rinv_rdy.at(l, v + 1))
                        A(cat[:, t, h * HD:(h + 1) * HD], bank(6 + v % 2, HD), ACT.Copy,
                          scale=rinv[:, v % 4:v % 4 + 1]).then_inc(o_ev.sem, 1)
                act.wait_ge(g1_ps.sem, g1_ps.at(l, 1))
                A(g1b[:, 0, :], PS[:, 0:1024], ACT.Copy)
                A(g1b[:, 1, :], PS[:, 1024:2048], ACT.Copy).then_inc(g1_rdy.sem, 1)
                sn = lambda j, s: vp[:, R_SN + j - 4:R_SN + j - 3] if j >= 4 else None
                move_groups(l, 1, sn, lambda j, s: None)
                for t in range(NT):
                    act.wait_ge(x2_rdy.sem, x2_rdy.at(l, t + 1))
                    squares(l, 2, t, xr[:, t, :], junk)
                    act.dma_start(x_res[t * P:(t + 1) * P, :], xr[:, t, :]).then_inc(stored.sem, 16)
                    if t:
                        act.wait_ge(xn_rdy.sem, xn_rdy.at(l, 2 * NT + t))
                        act.dma_start(xn_dram[(t - 1) * P:t * P, :], x_t[:, t - 1, :]).then_inc(stored.sem, 16)
                act.wait_ge(xn_rdy.sem, xn_rdy.at(l, 3 * NT))
                act.dma_start(xn_dram[(NT - 1) * P:NT * P, :], x_t[:, NT - 1, :]).then_inc(stored.sem, 16)
                move_groups(l, 2, lambda j, s: amp2[:, j, s:s + 1], lambda j, s: mod[:, 24 + j, s:s + 1])
                act.wait_ge(lg_sub.sem, lg_sub.at(l, 1))
                A(aff[:, :, :], aff[:, :, :], ACT.Exp).then_inc(lg_e.sem, 1)
                act.wait_ge(g2_ps.sem, g2_ps.at(l, 1))
                act.wait_ge(stored.sem, stored.at(l, 2 * NT))
                A(g2r[0:CAP_L, :], PS[0:CAP_L, 1024:2048], ACT.Copy)
                A(g2r[CAP_L:SLOT, :], PS[CAP_L:SLOT, 0:1024], ACT.Copy).then_inc(g2_rdy.sem, 1)
                act_gate_up(l * EXP, True, {3: lambda: tokens_high(l * EXP)})
                with act.Fori(1, EXP) as e:
                    E = l * EXP + e
                    act_down(E - 1, {4: lambda: tokens_high(E)})
                    act_gate_up(E, False, {4: lambda: rows_out(E - 1)})
                act_down(l * EXP + EXP - 1, {})
                rows_out(l * EXP + EXP - 1)

        @block.vector
        def _(dve):
            V = nc.vector
            chain = Chain(dve, "dve_chain", DVE_LINKS)
            first = Chain(dve, "dve_first", DVE_FIRST)
            loop = Chain(dve, "dve_loop", DVE_LOOP)
            link = chain.link

            def also(sig, ins, l, n):
                ins.then_inc(sig.sem, 1)
                dve.wait_ge(sig.sem, sig.at(l, n))

            def mean_eps(l, use, t, width):
                i = use * NT + t
                dve.wait_ge(ss_rdy.sem, ss_rdy.at(l, i + 1))
                V.tensor_scalar(rs[:, use, t:t + 1], ss[:, use, t:t + 1], 1.0 / width, EPS, ALU.mult, ALU.add).then_inc(u_rdy.sem, 1)

            def normed(l, use, t, out, src):
                i = use * NT + t
                dve.wait_ge(rstd_rdy.sem, rstd_rdy.at(l, i + 1))
                V.tensor_scalar(out, src, rs[:, use, t:t + 1], None, ALU.mult).then_inc(xn_rdy.sem, 1)

            def move_groups(l, use, amp, shift):
                for g in range(0, 10, 2):
                    dve.wait_ge(tg_ps.sem, tg_ps.at(l, use * 10 + g + 1))
                    b = bank(((0, 4, 0)[use] + g) % 8)
                    if g < 8:
                        put(hT[:, g, CTX:TOK], b, amp(g, 1), shift(g, 1)).then_inc(tg_dve.sem, 1)
                    else:
                        for i in range(4):
                            last = put(hT[:, i, 0:CTX], b[:, i * P:(i + 1) * P], amp(i, 0), shift(i, 0))
                        last.then_inc(tg_dve.sem, 1)

            def put(out, in_, a, s):
                if a is None:
                    return V.tensor_copy(out, in_)
                if s is None:
                    return V.tensor_scalar(out, in_, a, None, ALU.mult)
                return V.tensor_scalar(out, in_, a, s, ALU.mult, ALU.add)

            def column(ch, l, e, i, out, sig):
                ins = V.tensor_scalar(out, col[:, i, bass.ds(e, 1)] if not isinstance(e, int) else col[:, i, e:e + 1],
                                      1.0, None, ALU.mult)
                if sig:
                    ins.then_inc(sig.sem, 1)

            def tokens_in(ch, E):
                dve.wait_ge(xT_ps.sem, E + 1)
                rows = PS[:, 3072:4096].rearrange("p (b c) -> p b c", b=2)[:, :, 0:320].rearrange("p b (j s) -> p b j s", s=SLOT)
                for i, (m, op) in enumerate(((amp2[:, :, :], ALU.mult), (mod[:, 24:32, :], ALU.add))):
                    for st, a, n in ((1, 0, CAP_L), (0, CAP_L, CAP_C)):
                        v = m[:, :, st:st + 1].rearrange("p (b j) s -> p b j s", b=2).broadcast_to([P, 2, 4, n])
                        ins = V.tensor_tensor(rows[:, :, :, a:a + n], rows[:, :, :, a:a + n], v, op)
                    if i == 0:
                        ch.link(ins)
                ins.then_inc(xm_rdy.sem, 1)

            def tokens_low(E):
                dve.wait_ge(xh_rdy.sem, E + 1)
                V.tensor_tensor(xel[:, :, :].rearrange("p (b j) s -> p b (j s)", b=2),
                                PS[:, 3072:4096].rearrange("p (b c) -> p b c", b=2)[:, :, 0:320],
                                xeh[:, :, :].bitcast(F32).rearrange("p (b j) s -> p b (j s)", b=2), ALU.subtract).then_inc(xl_rdy.sem, 1)

            def times_up(E, n):
                dve.wait_ge(sg_rdy.sem, 2 * E + (n + 1))
                dve.wait_ge(slab_used.sem, 24 * E + (12 + 4 * n))
                h_ = hid[:, n * 512:(n + 1) * 512]
                V.tensor_tensor(h_, h_, PS[0:SLOT, (2 + n) * 512:(3 + n) * 512], ALU.mult).then_inc(hm_rdy.sem, 1)

            def hidden_low(E, n):
                dve.wait_ge(hh_rdy.sem, 2 * E + (n + 1))
                r_ = slice(4 * n, 4 * n + 4)
                V.tensor_tensor(hdl[:, r_, :].rearrange("p j s -> p (j s)"), PS[:, (2 + n) * 512:(2 + n) * 512 + 320],
                                hdh[:, r_, :].bitcast(F32).rearrange("p j s -> p (j s)"), ALU.subtract).then_inc(hl_rdy.sem, 1)

            def rest(E, j, i):
                if i not in DVE_SLABS:
                    return
                dve.wait_ge(hi_rdy.sem, 24 * E + (8 * j + i + 1))
                src, _ = slab(j, i)
                V.tensor_tensor(two(wl[:, i, :]), src, two(wh[:, i, :].bitcast(F32)), ALU.subtract).then_inc(lo_dve.sem, 1)

            def dve_down(ch, l, e, E, at):
                for i in range(8):
                    rest(E, 2, i)
                    if i == 0:
                        dve.wait_ge(landed.sem, E + 1)
                        column(ch, l, e, 1, idx_s[:, :], None)
                        column(ch, l, e, 0, gcur[:, :], idxs_rdy)
                    if i == 1:
                        hidden_low(E, 0)
                    if i == 2:
                        times_up(E, 1)
                    if i in at:
                        at[i]()
                    if i == 6:
                        hidden_low(E, 1)

            def dve_gate_up(ch, l, e, E, at):
                for i in range(16):
                    rest(E, i // 8, i % 8)
                    if i in at:
                        at[i]()
                    if i == 3:
                        column(ch, l, e + 1, 1, idx_g[:, :], idx_rdy)
                    if i == 14:
                        times_up(E, 0)

            for sem in primes:
                V.memset(hold[:, :], 0.0).then_inc(sem, 1)
                dve.wait_ge(sem, 1)
            V.memset(ones[:, :], 1.0).then_inc(dve_consts, 1)
            V.memset(mhalf[:, :], -0.5).then_inc(dve_consts, 1)
            V.memset(top[:, :, :], 0.0).then_inc(dve_consts, 1)
            V.memset(col[:, :, EXP:EXP + 1], 0.0).then_inc(dve_consts, 1)
            dve.wait_ge(dve_consts, 4)
            dve.wait_ge(rope_in, 16)
            dve.wait_ge(pool_consts, 8)
            with each_layer(dve) as l:
                chain.start(l)
                dve.wait_ge(vec_ps.sem, vec_ps.at(l, 1))
                also(vp_rdy, V.tensor_copy(vp[:, :], bank(0, VROWS)), l, 1)
                V.memset(xin[:, :, 0:2], 0.0)
                V.memset(xin[:, :, 2 + CTX:CW + 2], 0.0)
                V.memset(xin[:, :, CW + 2 + LAT:XL], 0.0).then_inc(pads.sem, 1)
                V.memset(mrows, 0.0).then_inc(rows0.sem, 1)
                for t in range(NT):
                    mean_eps(l, 0, t, D)
                for t in range(NT):
                    normed(l, 0, t, x_t[:, t, :], x_t[:, t, :])
                dve.wait_ge(ada_used.sem, ada_used.at(l, 8))
                dve.wait_ge(rows0.sem, rows0.at(l, 1))
                for q in (2, 3):
                    ins = V.tensor_copy(mrows[32 * q:32 * q + 2, :, :], PS[32 * q:32 * q + 2, 512:2048].rearrange("p (b c) -> p b c", b=3))
                ins.then_inc(rows_dve.sem, 1)
                dve.wait_ge(mod_ps.sem, mod_ps.at(l, 1))
                for b in range(3):
                    src = bank(4 + b).rearrange("p (i q c) -> p q i c", i=4, q=4)[:, :, :, 0:2]
                    ins = V.tensor_tensor(mod[:, 16 * b:16 * b + 16, :].rearrange("p (q i) s -> p q i s", q=4), src,
                                          vp[:, 16 * b:16 * b + 16].rearrange("p (q i) -> p q i", q=4).unsqueeze(3).broadcast_to([P, 4, 4, 2]), ALU.add)
                link(ins)
                V.scalar_tensor_tensor(amp1[:, :, :], mod[:, 8:16, :], 1.0,
                                       vp[:, R_N1:R_N1 + 8].unsqueeze(2).broadcast_to([P, 8, 2]), ALU.add, ALU.mult)
                also(mod_rdy, V.scalar_tensor_tensor(amp2[:, :, :], mod[:, 32:40, :], 1.0,
                                                     vp[:, R_N2:R_N2 + 8].unsqueeze(2).broadcast_to([P, 8, 2]), ALU.add, ALU.mult), l, 1)
                move_groups(l, 0, lambda j, s: amp1[:, j, s:s + 1], lambda j, s: mod[:, j, s:s + 1])

                for c in range(NC_):
                    dve.wait_ge(tap0.sem, tap0.at(l, c + 1))
                    for w in range(1, CONV_W):
                        r_ = R_CW + w * NC_ + c
                        ins = V.scalar_tensor_tensor(cv[:, c, :], xin[:, c, w:w + CL], vp[:, r_:r_ + 1], cv[:, c, :], ALU.mult, ALU.add)
                        if w < CONV_W - 1:
                            link(ins)
                    ins.then_inc(conv_rdy.sem, 1)

                dve.wait_ge(ip_ev.sem, ip_ev.at(l, 17))
                link(V.tensor_tensor(dtr[:, :, :], dtr[:, :, :], bp[:, B_DTB:B_DTB + 16].unsqueeze(1).broadcast_to([P, NT, 16]), ALU.add))
                link(V.tensor_scalar(dts[:, :, :], dtr[:, :, :], -1.0, None, ALU.mult))
                also(dt_abs, V.tensor_tensor(dts[:, :, :], dts[:, :, :], dtr[:, :, :], ALU.max), l, 1)
                for t in range(NT):
                    dve.wait_ge(qs_rdy.sem, qs_rdy.at(l, t + 1))
                    V.tensor_reduce(hs[:, t, 0:8], RA[:, t * 512:(t + 1) * 512].rearrange("p (h d) -> p h d", d=HD), AX.X, ALU.add)
                dve.wait_ge(qs_rdy.sem, qs_rdy.at(l, 6))
                ksq = RA[:, 2560:3200].rearrange("p (t h d) -> p t h d", t=NT, h=KVH)
                link(V.tensor_reduce(hs[:, :, 8:10], ksq, AX.X, ALU.add))
                V.tensor_scalar(hs[:, :, :], hs[:, :, :], 1.0 / HD, EPS, ALU.mult, ALU.add).then_inc(hsu_rdy.sem, 1)
                dve.wait_ge(hrs_rdy.sem, hrs_rdy.at(l, 1))
                k4 = kv_t[:, :, 0:P].rearrange("p t (h d) -> p t h d", h=KVH)
                for h in range(KVH):
                    kh = k4[:, :, h, :]
                    link(V.tensor_tensor(kh, kh, hs[:, :, 8 + h:9 + h].broadcast_to([P, NT, HD]), ALU.mult))
                    link(V.tensor_tensor(kh, kh, bp[:, B_KN:B_KN + HD].unsqueeze(1).broadcast_to([P, NT, HD]), ALU.mult))
                    lo, hi = kh[:, :, 0:32], kh[:, :, 32:64]
                    co, si = ropes[:, :, 0:32], ropes[:, :, 32:64]
                    tm = [RA[:, 3200 + i * 160:3360 + i * 160].rearrange("p (t d) -> p t d", t=NT) for i in range(4)]
                    V.tensor_tensor(tm[0], lo, co, ALU.mult)
                    V.tensor_tensor(tm[1], hi, si, ALU.mult)
                    V.tensor_tensor(tm[2], hi, co, ALU.mult)
                    link(V.tensor_tensor(tm[3], lo, si, ALU.mult))
                    V.tensor_tensor(lo, tm[0], tm[1], ALU.subtract)
                    ins = V.tensor_tensor(hi, tm[2], tm[3], ALU.add)
                    if h == KVH - 1:
                        ins.then_inc(k_rdy.sem, 1)
                link(V.tensor_scalar(bp[:, B_QN:B_QN + HD], bp[:, B_QN:B_QN + HD], HD ** -0.5, None, ALU.mult))
                for t in range(NT):
                    qh = q_t[:, t, :].rearrange("p (h d) -> p h d", h=HEADS)
                    link(V.tensor_tensor(qh, qh, hs[:, t, 0:8].unsqueeze(2).broadcast_to([P, 8, HD]), ALU.mult))
                    link(V.tensor_tensor(qh, qh, bp[:, B_QN:B_QN + HD].unsqueeze(1).broadcast_to([P, 8, HD]), ALU.mult))
                    lo, hi = qh[:, :, 0:32], qh[:, :, 32:64]
                    co = ropes[:, t, 0:32].unsqueeze(1).broadcast_to([P, 8, 32])
                    si = ropes[:, t, 32:64].unsqueeze(1).broadcast_to([P, 8, 32])
                    tm = [RA[:, 3840 + i * 256:4096 + i * 256].rearrange("p (h d) -> p h d", h=8) for i in range(4)]
                    V.tensor_tensor(tm[0], lo, co, ALU.mult)
                    V.tensor_tensor(tm[1], hi, si, ALU.mult)
                    V.tensor_tensor(tm[2], hi, co, ALU.mult)
                    link(V.tensor_tensor(tm[3], lo, si, ALU.mult))
                    V.tensor_tensor(lo, tm[0], tm[1], ALU.subtract)
                    V.tensor_tensor(hi, tm[2], tm[3], ALU.add).then_inc(q_rdy.sem, 1)
                dve.wait_ge(dt_e.sem, dt_e.at(l, 1))
                link(V.tensor_scalar(dts[:, :, :], dte[:, :, :], 2.0, None, ALU.add))
                link(V.reciprocal(dts[:, :, :], dts[:, :, :]))
                link(V.tensor_tensor(dts[:, :, :], dts[:, :, :], dte[:, :, :], ALU.mult))
                link(V.tensor_tensor(dte[:, :, :], dts[:, :, :], dts[:, :, :], ALU.mult))
                link(V.tensor_scalar(dt_[:, :, :], dte[:, :, :], 1.0 / 15, None, ALU.mult))
                for d in (13, 11, 9, 7, 5, 3):
                    link(V.scalar_tensor_tensor(dt_[:, :, :], dt_[:, :, :], 1.0 / d, dte[:, :, :], ALU.add, ALU.mult))
                link(V.scalar_tensor_tensor(dt_[:, :, :], dt_[:, :, :], 1.0, dts[:, :, :], ALU.add, ALU.mult))
                link(V.tensor_scalar(dtr[:, :, :], dtr[:, :, :], 0.0, None, ALU.max))
                link(V.scalar_tensor_tensor(dt_[:, :, :], dt_[:, :, :], 2.0, dtr[:, :, :], ALU.mult, ALU.add))
                V.scalar_tensor_tensor(adt[:, :, :], dt_[:, :, :], -1.0, negA[:, :].unsqueeze(1).broadcast_to([P, NT, 16]),
                                       ALU.mult, ALU.mult).then_inc(a_rdy.sem, 1)

                dve.wait_ge(cs_ps.sem, cs_ps.at(l, 1))
                link(V.tensor_copy(cs[:, :, :, :].rearrange("p a t h -> p (a t h)"), PS[:, 0:160]))
                V.tensor_scalar(ncs[:, :, :, :], cs[:, 0:2, :, :], -1.0, None, ALU.mult)
                V.tensor_tensor(wend[:, :, :, :], cs[:, 2:4, :, :], cs[:, 0:2, :, :], ALU.subtract).then_inc(cs_rdy.sem, 1)
                dve.wait_ge(cs_e.sem, cs_e.at(l, 1))
                for g in range(2):
                    rows = slice(g * HD, (g + 1) * HD)
                    for s in range(1, 4):
                        for r, t in ((0, F_STEP[s]), (1, B_STEP[s])):
                            V.tensor_copy(cds[rows, s - 1, r, :], etot[rows, r, t, g * GQ:(g + 1) * GQ])
                V.tensor_tensor(wend[:, :, :, :], wend[:, :, :, :], dt_[:, :, :].rearrange("p t (r h) -> p r t h", r=2),
                                ALU.mult).then_inc(wend_rdy.sem, 1)
                dve.wait_ge(h0_ps.sem, h0_ps.at(l, 1))
                dve.wait_ge(tok_ps.sem, tok_ps.at(l, NT))
                link(V.tensor_copy(hprev[:, 0, :, :].rearrange("p r c -> p (r c)"), bank(1)))
                for s in range(4):
                    dve.wait_ge(S_ps.sem, S_ps.at(l, s + 1))
                    if s == 0:
                        V.tensor_copy(hctx.rearrange("p r c -> p (r c)"), bank(4)).then_inc(h_rdy.sem, 1)
                        continue
                    dcy = cds[:, s - 1, :, :].rearrange("p r h -> p (r h)").unsqueeze(2).broadcast_to([P, 8, HD])
                    old = hprev[:, s - 1, :, :].rearrange("p r (h c) -> p (r h) c", c=HD)
                    new = hprev[:, s, :, :].rearrange("p r (h c) -> p (r h) c", c=HD)
                    link(V.tensor_tensor(new, old, dcy, ALU.mult))
                    also(h_rdy, V.tensor_tensor(new, new, bank(4 + s).rearrange("p (h c) -> p h c", c=HD), ALU.add), l, s + 1)

                def exponents(t):
                    for r in range(2):
                        dve.wait_ge(seg_ps.sem, seg_ps.at(l, 2 * t + r + 1))
                        if t:
                            dve.wait_ge(yd_ps.sem, yd_ps.at(l, 2 * (t - 1) + r + 1))
                        for h in range(8):
                            o = (2 + 2 * r) * 512 + h * P
                            ins = V.scalar_tensor_tensor(EW[:, r, h * P:(h + 1) * P], PS[:, o:o + P], ncs[:, r, t, h:h + 1],
                                                         bars[:, r, :], ALU.add, ALU.min)
                        ins.then_inc(m_rdy.sem, 1)

                def weights(t):
                    for r in range(2):
                        dve.wait_ge(e_rdy.sem, e_rdy.at(l, 2 * t + r + 1))
                        for g in range(2):
                            e_ = EW[:, r, g * 512:(g + 1) * 512].rearrange("p (h i) -> p h i", h=GQ)
                            o = g * P
                            ins = V.tensor_tensor(e_, e_, PS[:, o:o + P].unsqueeze(1).broadcast_to([P, GQ, P]), ALU.mult)
                        ins.then_inc(w_rdy.sem, 1)

                dve.wait_ge(S_ps.sem, S_ps.at(l, 4))
                exponents(0)
                for t in range(NT):
                    dve.wait_ge(G_ps.sem, G_ps.at(l, 2 * t + 2))
                    weights(t)
                    if t + 1 < NT:
                        exponents(t + 1)
                    y = cat[:, t, 512:1024]
                    byhead = lambda a: a.rearrange("p (h c) -> p h c", c=HD)
                    dve.wait_ge(yd_ps.sem, yd_ps.at(l, 2 * t + 2))
                    dve.wait_ge(skip_rdy.sem, skip_rdy.at(l, t + 1))
                    link(V.tensor_tensor(y, bank(1), xskip[:, t % 2, :], ALU.add))
                    if t:
                        dve.wait_ge(y_ps.sem, y_ps.at(l, t))
                        for r in range(2):
                            off = PS[:, 3072:4096].rearrange("p (g r c) -> p g r c", g=2, r=2)[:, :, r, :].rearrange("p g (h c) -> p g h c", c=HD)
                            link(V.tensor_tensor(ytmp.rearrange("p (g h c) -> p g h c", g=2, c=HD), off,
                                                 ecs[:, r, t, :].rearrange("p (g h) -> p g h", g=2).unsqueeze(3).broadcast_to([P, 2, GQ, HD]), ALU.mult))
                            link(V.tensor_tensor(y, y, ytmp, ALU.add))
                    V.tensor_tensor(y, y, z_t[:, t, :], ALU.mult).then_inc(y_done.sem, 1)
                for t in range(NT):
                    mean_eps(l, 1, t, 512)
                for t in range(3):
                    dve.wait_ge(qkT_ps.sem, qkT_ps.at(l, t + 2))
                    V.tensor_copy(qT[:, :, t * P:(t + 1) * P], bank(2 + t).rearrange("p (m s) -> p m s", m=GQ)).then_inc(qkT_dve.sem, 1)
                for u in range(UN + 1):
                    if u < UN:
                        n_ = 640 if u >= HEADS else P
                        dve.wait_ge(s_ps.sem, s_ps.at(l, u + 1))
                        if u >= 4:
                            dve.wait_ge(p_rdy.sem, p_rdy.at(l, u - 3))
                        V.tensor_reduce(nmax[:, u % 4:u % 4 + 1], PS[:, (u % 2) * 1024:(u % 2) * 1024 + n_], AX.X, ALU.max,
                                        negate=True).then_inc(max_rdy.sem, 1)
                    if u:
                        v = u - 1
                        n_ = 640 if v >= HEADS else P
                        dve.wait_ge(p_rdy.sem, p_rdy.at(l, v + 1))
                        if v >= 4:
                            dve.wait_ge(o_ev.sem, o_ev.at(l, v - 3))
                        V.reciprocal(rinv[:, v % 4:v % 4 + 1], psum_[:, v % 4:v % 4 + 1]).then_inc(rinv_rdy.sem, 1)
                        dve.wait_ge(t_ps.sem, t_ps.at(l, v + 1))
                        if v >= 2:
                            dve.wait_ge(o_ps.sem, o_ps.at(l, v - 1))
                        V.tensor_copy(pT[:, v % 2, 0:n_], PS[:, 2048:2048 + n_]).then_inc(pT_rdy.sem, 1)
                    if u in (8, 16, 24, 32, 36):
                        t = (8, 16, 24, 32, 36).index(u)
                        normed(l, 1, t, cat[:, t, 512:1024], cat[:, t, 512:1024])
                sn = lambda j, s: vp[:, R_SN + j - 4:R_SN + j - 3] if j >= 4 else None
                move_groups(l, 1, sn, lambda j, s: None)
                dve.wait_ge(x2_in.sem, x2_in.at(l, 1))
                dve.wait_ge(g1_rdy.sem, g1_rdy.at(l, 1))
                for t in range(NT):
                    dve.wait_ge(op_ps.sem, op_ps.at(l, t + 1))
                    also(op_ev, V.tensor_tensor(optmp, PS[:, (t % 4) * 1024:(t % 4) * 1024 + 1024], g1b[:, 1 if t else 0, :], ALU.mult), l, t + 1)
                    also(x2_rdy, V.tensor_tensor(xr[:, t, :], xr[:, t, :], optmp, ALU.add), l, t + 1)
                    if t:
                        mean_eps(l, 2, t - 1, D)
                        normed(l, 2, t - 1, x_t[:, t - 1, :], xr[:, t - 1, :])
                mean_eps(l, 2, NT - 1, D)
                normed(l, 2, NT - 1, x_t[:, NT - 1, :], xr[:, NT - 1, :])
                move_groups(l, 2, lambda j, s: amp2[:, j, s:s + 1], lambda j, s: mod[:, 24 + j, s:s + 1])

                dve.wait_ge(lg_ps.sem, lg_ps.at(l, 1))
                lg = PS[:, 1024:1024 + NT * EXP].rearrange("p (t e) -> p t e", t=NT)
                wide = am[:, :].unsqueeze(2).broadcast_to([P, NT, EXP])
                link(V.tensor_reduce(am[:, :], lg, AX.X, ALU.max))
                V.tensor_tensor(aff[:, :, :], lg, wide, ALU.subtract).then_inc(lg_sub.sem, 1)
                dve.wait_ge(lg_e.sem, lg_e.at(l, 1))
                link(V.tensor_reduce(am[:, :], aff[:, :, :], AX.X, ALU.add))
                link(V.reciprocal(am[:, :], am[:, :]))
                V.tensor_tensor(aff[:, :, :], aff[:, :, :], wide, ALU.mult).then_inc(aff_rdy.sem, 1)
                dve.wait_ge(affT_ps.sem, affT_ps.at(l, 1))
                link(V.tensor_copy(wa, PS[0:EXP, 2048:2048 + TOK]))
                V.memset(hold[:, :], 0.0)
                for st, a, n, rounds, s0 in ((1, CTX, LAT, CAP_L // 8, 0), (0, 0, CTX, CAP_C // 8, CAP_L)):
                    cur, nxt = wa, wb
                    for i in range(rounds):
                        o = s0 + 8 * i
                        link(V.max(top[0:EXP, 0, o:o + 8], cur[:, a:a + n]))
                        V.memset(hold[:, :], 0.0)
                        if i + 1 < rounds:
                            ins = V.match_replace(nxt[:, a:a + n], top[0:EXP, 0, o:o + 8], cur[:, a:a + n], -1.0)
                            V.max_index(topu[:, o:o + 8], top[0:EXP, 0, o:o + 8], cur[:, a:a + n])
                            link(ins)
                            V.memset(hold[:, :], 0.0)
                        else:
                            link(V.max_index(topu[:, o:o + 8], top[0:EXP, 0, o:o + 8], cur[:, a:a + n]))
                            V.memset(hold[:, :], 0.0)
                        cur, nxt = nxt, cur
                V.tensor_scalar(top[0:EXP, 1, 0:CAP_L], topu[:, 0:CAP_L], float(CTX), None, ALU.add)
                V.tensor_scalar(top[0:EXP, 1, CAP_L:SLOT], topu[:, CAP_L:SLOT], 0.0, None, ALU.add).then_inc(top_rdy.sem, 1)
                dve.wait_ge(col_ps.sem, col_ps.at(l, 1))
                also(col_rdy, V.tensor_copy(col[:, :, 0:EXP], PS[0:SLOT, 3072:3328].rearrange("p (i e) -> p i e", i=2)[:, :, 0:EXP]), l, 1)
                chain.end()

                E = l * EXP
                first.start(l)
                column(first, l, 0, 1, idx_g[:, :], idx_rdy)
                dve_gate_up(first, l, 0, E, {1: lambda: tokens_in(first, E), 3: lambda: tokens_low(E)})
                first.end()
                with dve.Fori(1, EXP) as e:
                    E = l * EXP + e
                    loop.start(l * (EXP - 1) + e - 1)
                    dve_down(loop, l, e - 1, E - 1, {3: lambda: tokens_in(loop, E), 5: lambda: tokens_low(E)})
                    dve_gate_up(loop, l, e, E, {})
                    loop.end()
                E = l * EXP + EXP
                dve_down(None, l, EXP - 1, E - 1, {})

        @block.gpsimd
        def _(pool):
            G = nc.gpsimd
            TT = G.tensor_tensor

            def hold_here(before):
                pool.wait_ge(held.sem, before)
                TT(pgate[:, 0:1], pgate[:, 0:1], pgate[:, 0:1], ALU.add).then_inc(held.sem, 1)

            G.memset(pgate[:, :], 0.0).then_inc(pool_consts, 1)
            G.memset(ident[:, :], 0.0).then_inc(pool_consts, 1)
            pool.wait_ge(pool_consts, 2)
            pool.wait_ge(dve_consts, 4)
            G.affine_select(out=ident[:, :], in_=ident[:, :], compare_op=ALU.not_equal, fill=1.0, base=0,
                            pattern=[[-1, P]], channel_multiplier=1).then_inc(pool_consts, 1)
            G.affine_select(out=upto[:, :], in_=ones[:, :], compare_op=ALU.is_ge, fill=0.0, base=0,
                            pattern=[[1, P]], channel_multiplier=-1).then_inc(pool_consts, 1)
            G.affine_select(out=since[:, :], in_=ones[:, :], compare_op=ALU.is_ge, fill=0.0, base=0,
                            pattern=[[-1, P]], channel_multiplier=1).then_inc(pool_consts, 1)
            G.memset(bars[:, :, :], 0.0).then_inc(pool_consts, 1)
            pool.wait_ge(pool_consts, 6)
            for r in range(2):
                G.affine_select(out=bars[:, r, :], in_=bars[:, r, :], compare_op=ALU.is_ge, fill=-1e30, base=0,
                                pattern=[[1 - 2 * r, P]], channel_multiplier=2 * r - 1).then_inc(pool_consts, 1)
            pool.wait_ge(pool_consts, 8)

            def root(l, use, t):
                i = use * NT + t
                pool.wait_ge(u_rdy.sem, u_rdy.at(l, i + 1))
                TT(rs[:, use, t:t + 1], rs[:, use, t:t + 1], mhalf[:, 0:1], ALU.pow).then_inc(rstd_rdy.sem, 1)

            def gather():
                G.indirect_dma_start(out=xg, out_offset=None, in_=xn_dram[:, :],
                                     in_offset=bass.IndirectOffsetOnAxis(ap=idx_g[:, 0:1], axis=0),
                                     ).then_inc(gathered.sem, 16)

            def scatter(E, before):
                pool.wait_ge(ys_rdy.sem, E + 1)
                hold_here(before)
                G.indirect_dma_start(out=x_res[:, :], out_offset=bass.IndirectOffsetOnAxis(ap=idx_s[:, 0:1], axis=0),
                                     in_=ys, in_offset=None, compute_op=ALU.add).then_inc(scattered.sem, 16)

            def land(E):
                pool.wait_ge(scattered.sem, E * 16 + 16)
                pool.wait_ge(landed.sem, E + 1)
                TT(pgate[:, 1:2], pgate[:, 1:2], pgate[:, 1:2], ALU.add).then_inc(landed.sem, 1)

            def rest(E, j, i):
                if i not in POOL_SLABS:
                    return
                pool.wait_ge(hi_rdy.sem, 24 * E + (8 * j + i + 1))
                src, _ = slab(j, i)
                TT(two(wl[:, i, :]), src, two(wh[:, i, :].bitcast(F32)), ALU.subtract).then_inc(lo_pool.sem, 1)

            def gate2(E):
                pool.wait_ge(d_ev.sem, E + 2)
                TT(ys, ys, g2r, ALU.mult).then_inc(ys_rdy.sem, 1)

            with each_layer(pool) as l:
                for t in range(NT):
                    root(l, 0, t)
                for t in range(NT):
                    pool.wait_ge(ip_ev.sem, ip_ev.at(l, 18 + t))
                    TT(RA[:, t * 512:(t + 1) * 512], q_t[:, t, :], q_t[:, t, :], ALU.mult).then_inc(qs_rdy.sem, 1)
                TT(RA[:, 2560:3200].rearrange("p (t c) -> p t c", t=NT), kv_t[:, :, 0:P], kv_t[:, :, 0:P], ALU.mult).then_inc(qs_rdy.sem, 1)
                pool.wait_ge(hsu_rdy.sem, hsu_rdy.at(l, 1))
                TT(hs[:, :, :].rearrange("p t h -> p (t h)"), hs[:, :, :].rearrange("p t h -> p (t h)"), mhalf[:, :], ALU.pow).then_inc(hrs_rdy.sem, 1)
                byhead = lambda a: a.rearrange("p (h c) -> p h c", c=HD)
                pool.wait_ge(wend_rdy.sem, wend_rdy.at(l, 1))
                pool.wait_ge(tok_ev.sem, tok_ev.at(l, NT))
                pool.wait_ge(q_rdy.sem, q_rdy.at(l, NT))
                for s in range(4):
                    for r, t in ((0, F_STEP[s]), (1, B_STEP[s])):
                        last = TT(byhead(xw[s][:, r * 512:(r + 1) * 512]), byhead(tokx[:, t, 0:512]),
                                  wend[:, r, t, :].unsqueeze(2).broadcast_to([P, 8, HD]), ALU.mult)
                    last.then_inc(xw_rdy.sem, 1)
                pool.wait_ge(S_ps.sem, S_ps.at(l, 4))
                for t in range(NT):
                    for r in range(2):
                        if t:
                            pool.wait_ge(yd_ps.sem, yd_ps.at(l, 2 * (t - 1) + r + 1))
                        TT(byhead(xdt[:, r, :]), byhead(tokx[:, t, 0:512]),
                           dt_[:, t, r * 8:(r + 1) * 8].unsqueeze(2).broadcast_to([P, 8, HD]), ALU.mult).then_inc(xdt_rdy.sem, 1)
                    if t >= 2:
                        pool.wait_ge(y_done.sem, y_done.at(l, t - 1))
                    TT(byhead(xskip[:, t % 2, :]), byhead(tokx[:, t, 0:512]),
                       bp[:, B_SK:B_SK + 8].unsqueeze(2).broadcast_to([P, 8, HD]), ALU.mult).then_inc(skip_rdy.sem, 1)
                for t in range(NT):
                    root(l, 1, t)
                for t in range(NT):
                    root(l, 2, t)
                pool.wait_ge(stored.sem, stored.at(l, 2 * NT))
                pool.wait_ge(tg_ps.sem, tg_ps.at(l, 30))
                pool.wait_ge(idx_rdy.sem, idx_rdy.at(l, 1))
                hold_here(held.at(l, 0))
                gather()

                def next_gather(e, before):
                    pool.wait_ge(xT_ps.sem, l * EXP + (e + 1))
                    pool.wait_ge(idx_rdy.sem, idx_rdy.at(l, 2) + e)
                    hold_here(before)
                    gather()

                for i in range(16):
                    rest(l * EXP, i // 8, i % 8)
                    if i == 3:
                        next_gather(0, held.at(l, 1))
                with pool.Fori(1, EXP) as e:
                    E = l * EXP + e
                    for i in range(8):
                        rest(E - 1, 2, i)
                    for i in range(16):
                        rest(E, i // 8, i % 8)
                        if i == 3:
                            next_gather(e, held.at(l, 0) + 2 * e)
                        if i == 7:
                            gate2(E - 1)
                            scatter(E - 1, held.at(l, 1) + 2 * e)
                        if i == 15:
                            land(E - 1)
                for i in range(8):
                    rest(l * EXP + EXP - 1, 2, i)
                gate2(l * EXP + EXP - 1)
                scatter(l * EXP + EXP - 1, held.at(l, 2 * EXP))
                pool.wait_ge(gathered.sem, gathered.at(l, EXP + 1))
                land(l * EXP + EXP - 1)


SLAB = 1024
DVE_SLABS, POOL_SLABS = (0, 1, 2, 4, 5, 6), (3, 7)
DVE_LINKS, DVE_FIRST, DVE_LOOP = 108, 1, 1


def rope_table():
    t = np.arange(LAT)
    inv = (10000.0 ** (-np.arange(16, dtype=np.float32) / np.float32(16))).astype(np.float32)
    ang = np.concatenate([(t // GRID_W).astype(np.float32)[:, None] * inv,
                          (t % GRID_W).astype(np.float32)[:, None] * inv], axis=1)
    tab = np.zeros((TOK, 64), np.float32)
    tab[:, 0:32] = 1.0
    tab[CTX:, 0:32] = np.cos(ang)
    tab[CTX:, 32:64] = np.sin(ang)
    return np.ascontiguousarray(tab.reshape(NT, P, 64).transpose(1, 0, 2))


def kernel(**inputs):
    import concourse.bacc as bacc
    from concourse.bass_utils import run_bass_kernel_spmd

    a = {k: np.asarray(v) for k, v in inputs.items()}
    L = LAYERS
    both = lambda v: np.broadcast_to(v.reshape(1, 8, P), (L, 8, P))
    arrays = {
        "x_prompt": a["x_prompt"].reshape(CTX, D),
        "x_sample": a["x_sample"].reshape(LAT, D),
        "cache_k": a["cache_k"].reshape(L, P, P),
        "cache_v": a["cache_v"].reshape(L, P, P),
        "state": a["state_ssm"].reshape(L, 2, HEADS, HD, HD),
        "vrows": np.concatenate([
            a["ada_b"].reshape(L, 48, P), a["norm1"].reshape(L, 8, P), a["norm2"].reshape(L, 8, P),
            a["ssm_norm"].reshape(L, 4, P), a["conv_b"].reshape(L, NC_, P),
            a["conv_w"].reshape(L, CONV_W * NC_, P), both(a["c_ctx"]), both(a["c"])], axis=1),
        "bparams": np.concatenate([
            a["q_norm"], a["k_norm"], a["A_log"].reshape(L, 16), a["dt_bias"].reshape(L, 16), a["d_skip"]], axis=1),
        "rope": rope_table(),
        "ada_w": a["ada_w"], "w_in": a["w_in"], "w_out": a["w_out"], "w_router": a["w_router"],
        "w_gate": a["w_gate"].reshape(L * EXP, D, FF), "w_up": a["w_up"].reshape(L * EXP, D, FF),
        "w_down": a["w_down"].reshape(L * EXP, FF, D),
    }
    arrays = {k: np.ascontiguousarray(v) for k, v in arrays.items()}
    outs = {"x_res": (TOK, D), "new_k": (L, P, P), "new_v": (L, P, P), "new_h": (L, 2, HEADS, HD, HD)}
    nc = bacc.Bacc("TRN2", target_bir_lowering=False, num_devices=1)
    args = [nc.dram_tensor(k, v.shape, F32, kind="ExternalInput").ap() for k, v in arrays.items()]
    args += [nc.dram_tensor(k, s, F32, kind="ExternalOutput").ap() for k, s in outs.items()]
    build(nc, *args)
    r = run_bass_kernel_spmd(nc, [arrays], core_ids=[0]).results[0]
    x = np.asarray(r["x_res"])
    return (x[0:CTX].reshape(1, CTX, D), x[CTX:TOK].reshape(1, LAT, D),
            np.asarray(r["new_k"]).reshape(1, L, CTX, KVH, HD), np.asarray(r["new_v"]).reshape(1, L, CTX, KVH, HD),
            np.asarray(r["new_h"]).reshape(1, L, 2, HEADS, HD, HD))
```
